# Optimizing a Trainium2 kernel written in Bass

```python
import math
import jax, jax.numpy as jnp
from jax import lax
import numpy as np

D_MODEL = 2048
BATCH = 1
SEQ = 256
DEPTH = 2

CHUNK = 64
N_A_LAYERS = DEPTH // 2
N_B_LAYERS = DEPTH - N_A_LAYERS
S5_GROUP = 16
S5_GROUPS = D_MODEL // S5_GROUP
S5_STATE = 64
DT_MIN = 1e-3
DT_MAX = 1e-1
FOX_HEAD_DIM = 128
FOX_HEADS = D_MODEL // FOX_HEAD_DIM
Q_BLOCK = 128
FGATE_BIAS_LO = 1.0
FGATE_BIAS_HI = 6.0
D_FF = 5632
CONV_WIDTH = 3
NORM_EPS = 1e-6

kernel_name = "s5_fox_yoco_convglu_trunk"

def rms_norm(x, g):
    xf = x.astype(jnp.float32)
    y = xf * lax.rsqrt(jnp.mean(xf * xf, axis=-1, keepdims=True) + NORM_EPS)
    return (y * g.astype(jnp.float32)).astype(x.dtype)

def s5_mixer(h, w_in, lam_re, lam_im, log_step, b_re, b_im, c_re, c_im, d, w_glu):
    f32 = jnp.float32
    bsz, seq, _ = h.shape
    u = (h @ w_in).astype(f32).reshape(bsz, seq, S5_GROUPS, S5_GROUP)
    lam = lax.complex(lam_re.astype(f32), lam_im.astype(f32))
    dt = jnp.exp(log_step.astype(f32))[:, None]
    lam_bar = jnp.exp(lam * dt)
    b = lax.complex(b_re.astype(f32), b_im.astype(f32))
    b_bar = ((lam_bar - 1.0) / lam)[..., None] * b
    bu = jnp.einsum('blgc,gpc->blgp', u.astype(jnp.complex64), b_bar)
    a = jnp.broadcast_to(lam_bar, bu.shape)

    def combine(e1, e2):
        a1, s1 = e1
        a2, s2 = e2
        return a1 * a2, a2 * s1 + s2

    _, states = lax.associative_scan(combine, (a, bu), axis=1)
    c = lax.complex(c_re.astype(f32), c_im.astype(f32))
    y = jnp.real(jnp.einsum('blgp,gcp->blgc', states, c)) + d.astype(f32) * u
    y = jax.nn.gelu(y.reshape(bsz, seq, D_MODEL)).astype(h.dtype)
    val, gate = jnp.split(y @ w_glu, 2, axis=-1)
    return val * jax.nn.sigmoid(gate)

def fox_attention(h, w_q, w_o, k, v, logf_cum):
    bsz, seq, _ = h.shape
    n_blk = seq // Q_BLOCK
    q = (h @ w_q).reshape(bsz, n_blk, Q_BLOCK, FOX_HEADS, FOX_HEAD_DIM).transpose(1, 0, 2, 3, 4)
    cq = logf_cum.reshape(bsz, FOX_HEADS, n_blk, Q_BLOCK).transpose(2, 0, 1, 3)
    k_pos = jnp.arange(seq)
    scale = FOX_HEAD_DIM ** -0.5

    def block(args):
        qb, cqb, blk = args
        q_pos = blk * Q_BLOCK + jnp.arange(Q_BLOCK)
        s = jnp.einsum('bqhd,bkhd->bhqk', qb, k).astype(jnp.float32) * scale
        s = s + (cqb[..., :, None] - logf_cum[:, :, None, :])
        s = jnp.where(k_pos[None, :] <= q_pos[:, None], s, -jnp.inf)
        p = jax.nn.softmax(s, axis=-1)
        return jnp.einsum('bhqk,bkhd->bqhd', p.astype(v.dtype), v)

    o = lax.map(block, (q, cq, jnp.arange(n_blk)))
    o = o.transpose(1, 0, 2, 3, 4).reshape(bsz, seq, D_MODEL)
    return o @ w_o

def conv_glu_ffn(h, w_up, conv_w, conv_b, w_down):
    gate, val = jnp.split(h @ w_up, 2, axis=-1)
    gate = lax.conv_general_dilated(
        gate, conv_w[:, None, :], window_strides=(1,),
        padding=[(CONV_WIDTH - 1, 0)],
        dimension_numbers=('NWC', 'WIO', 'NWC'),
        feature_group_count=D_FF) + conv_b
    return (jax.nn.gelu(gate) * val) @ w_down

def setup_inputs(seed: int = 0) -> dict:
    key = jax.random.key(seed)
    ks = jax.random.split(key, 32)
    f32 = jnp.float32

    def nrm(k, shape, scale):
        return jax.random.normal(k, shape, f32) * scale

    na, nb, G, P, C, H = N_A_LAYERS, N_B_LAYERS, S5_GROUPS, S5_STATE, S5_GROUP, FOX_HEADS
    n_idx = jnp.arange(P, dtype=f32)
    return {
        "x": nrm(ks[0], (BATCH, SEQ, D_MODEL), 1.0),
        "a_norm": 1.0 + nrm(ks[1], (na, D_MODEL), 0.02),
        "a_w_in": nrm(ks[2], (na, D_MODEL, D_MODEL), D_MODEL ** -0.5),
        "a_lambda_re": -0.5 + nrm(ks[3], (na, G, P), 0.01),
        "a_lambda_im": math.pi * n_idx + nrm(ks[4], (na, G, P), 0.01),
        "a_log_step": jax.random.uniform(ks[5], (na, G), f32, math.log(DT_MIN), math.log(DT_MAX)),
        "a_b_re": nrm(ks[6], (na, G, P, C), (2 * C) ** -0.5),
        "a_b_im": nrm(ks[7], (na, G, P, C), (2 * C) ** -0.5),
        "a_c_re": nrm(ks[8], (na, G, C, P), (2 * P) ** -0.5),
        "a_c_im": nrm(ks[9], (na, G, C, P), (2 * P) ** -0.5),
        "a_d": nrm(ks[10], (na, G, C), 0.5),
        "a_w_glu": nrm(ks[11], (na, D_MODEL, 2 * D_MODEL), D_MODEL ** -0.5),
        "kv_norm": 1.0 + nrm(ks[12], (D_MODEL,), 0.02),
        "w_k": nrm(ks[13], (D_MODEL, D_MODEL), D_MODEL ** -0.5),
        "w_v": nrm(ks[14], (D_MODEL, D_MODEL), D_MODEL ** -0.5),
        "w_f": nrm(ks[15], (D_MODEL, H), D_MODEL ** -0.5),
        "b_f": jnp.linspace(FGATE_BIAS_LO, FGATE_BIAS_HI, H, dtype=f32) + nrm(ks[16], (H,), 0.1),
        "b_norm": 1.0 + nrm(ks[17], (nb, D_MODEL), 0.02),
        "b_w_q": nrm(ks[18], (nb, D_MODEL, D_MODEL), D_MODEL ** -0.5),
        "b_w_o": nrm(ks[19], (nb, D_MODEL, D_MODEL), D_MODEL ** -0.5),
        "ffn_norm": 1.0 + nrm(ks[20], (DEPTH, D_MODEL), 0.02),
        "ffn_w_up": nrm(ks[21], (DEPTH, D_MODEL, 2 * D_FF), D_MODEL ** -0.5),
        "ffn_conv_w": nrm(ks[22], (DEPTH, CONV_WIDTH, D_FF), CONV_WIDTH ** -0.5),
        "ffn_conv_b": nrm(ks[23], (DEPTH, D_FF), 0.01),
        "ffn_w_down": nrm(ks[24], (DEPTH, D_FF, D_MODEL), D_FF ** -0.5),
        "final_norm": 1.0 + nrm(ks[25], (D_MODEL,), 0.02),
    }

def reference(x, a_norm, a_w_in, a_lambda_re, a_lambda_im, a_log_step, a_b_re, a_b_im,
              a_c_re, a_c_im, a_d, a_w_glu, kv_norm, w_k, w_v, w_f, b_f, b_norm, b_w_q,
              b_w_o, ffn_norm, ffn_w_up, ffn_conv_w, ffn_conv_b, ffn_w_down, final_norm):
    bsz, seq, _ = x.shape
    for i in range(N_A_LAYERS):
        x = x + s5_mixer(rms_norm(x, a_norm[i]), a_w_in[i], a_lambda_re[i], a_lambda_im[i],
                         a_log_step[i], a_b_re[i], a_b_im[i], a_c_re[i], a_c_im[i], a_d[i],
                         a_w_glu[i])
        x = x + conv_glu_ffn(rms_norm(x, ffn_norm[i]), ffn_w_up[i], ffn_conv_w[i],
                             ffn_conv_b[i], ffn_w_down[i])
    h_kv = rms_norm(x, kv_norm)
    k = (h_kv @ w_k).reshape(bsz, seq, FOX_HEADS, FOX_HEAD_DIM)
    v = (h_kv @ w_v).reshape(bsz, seq, FOX_HEADS, FOX_HEAD_DIM)
    log_f = jax.nn.log_sigmoid((h_kv @ w_f + b_f).astype(jnp.float32))
    logf_cum = jnp.cumsum(log_f, axis=1).transpose(0, 2, 1)
    for j in range(N_B_LAYERS):
        li = N_A_LAYERS + j
        x = x + fox_attention(rms_norm(x, b_norm[j]), b_w_q[j], b_w_o[j], k, v, logf_cum)
        x = x + conv_glu_ffn(rms_norm(x, ffn_norm[li]), ffn_w_up[li], ffn_conv_w[li],
                             ffn_conv_b[li], ffn_w_down[li])
    return rms_norm(x, final_norm)


_drawn_inputs = setup_inputs


def setup_inputs(seed=0):
    import zlib

    import numpy as np

    out = dict(_drawn_inputs(seed))
    spreads = {}
    factors = {'a_norm': 8.0,
     'a_lambda_re': 8.0,
     'a_b_re': 3.452,
     'a_b_im': 3.497,
     'a_c_re': 3.519,
     'a_c_im': 3.463,
     'kv_norm': 7.546,
     'b_norm': 8.0,
     'ffn_conv_b': 7.195,
     'final_norm': 2.722}
    for name, (base, spread) in spreads.items():
        noise = np.random.default_rng([zlib.crc32(name.encode()), seed]).standard_normal(out[name].shape)
        drawn = base * np.exp(spread * noise) if base else spread * noise
        out[name] = __import__('jax').numpy.asarray(drawn.astype(out[name].dtype))
    for name, factor in factors.items():
        out[name] = (out[name] * factor).astype(out[name].dtype)
    return out
```

```python
from contextlib import ExitStack

import concourse.bass as bass
from concourse import mybir

ALU = mybir.AluOpType
ACT = mybir.ActivationFunctionType
AX_X = mybir.AxisListType.X
F32 = mybir.dt.float32
F32R = mybir.dt.float32r
I32 = mybir.dt.int32

P = 128
D_MODEL = 2048
SEQ = 256
D_FF = 5632
HEADS = 16
HEAD_DIM = 128
CONV_WIDTH = 3
NORM_EPS = 1e-6
STATE = 64
GROUP = 16
KT = D_MODEL // P
FT = D_FF // P
PAIRS = D_MODEL // GROUP // 2
UNIT_KT = 4
RING = 2
HALVES = 2
STRIP = 512
CHUNK = 64
CHUNKS = SEQ // CHUNK
SCALE = float(HEAD_DIM) ** -0.5
MASKED = -3.0e38
GAIN_A, GAIN_FFN0, GAIN_KV, GAIN_B, GAIN_FFN1, GAIN_FINAL = range(6)


class Phase:

    units = strips = scale_strips = fin_strips = up_strips = 0

    def __init__(self, kind, strips, kc, w, w0=0, norm=0, gain=None, layer=None, mul=1.0):
        self.kind, self.strips, self.kc = kind, strips, kc
        self.w, self.w0 = w, w0
        self.norm = norm
        self.gain = gain
        self.layer = layer
        self.mul = mul
        self.src = self.dst = None
        self.unit0, self.strip0 = Phase.units, Phase.strips
        self.scale0, self.fin0, self.up0 = Phase.scale_strips, Phase.fin_strips, Phase.up_strips
        Phase.units += strips * kc
        Phase.strips += strips
        Phase.scale_strips += strips * (kind == "scale")
        Phase.fin_strips += strips * (kind in ("glu", "fin"))
        Phase.up_strips += strips * (kind == "up")


class Chain:

    def __init__(self, eng, sem):
        self.eng, self.sem, self.base, self.local = eng, sem, 0, 0

    def step(self, ins):
        ins.then_inc(self.sem, 1)
        self.local += 1

    def wait(self):
        self.eng.wait_ge(self.sem, self.base + self.local)

    def enter(self, i, per):
        self.saved, self.base, self.local = self.base + self.local, self.base + self.local + i * per, 0

    def leave(self, rounds, per):
        assert self.local == per, (self.local, per)
        self.base, self.local = self.saved + rounds * per, 0


def trunk(nc, xT, gains, w_in, w_glu, w_k, w_v, w_f, b_f, w_q, w_o, w_up, w_down, conv, skip_d,
          lam, log_step, b_in, c_out, out):
    Phase.units = Phase.strips = Phase.scale_strips = Phase.up_strips = 0
    Phase.fin_strips = 4
    n_ffn_units = D_FF * 2 // STRIP * 4
    WIN = Phase("scale", 4, 4, w=w_in, w0=0, norm=1)
    GLU = Phase("glu", 8, 4, w=w_glu, w0=0, norm=0, gain=GAIN_FFN0)
    UP0 = Phase("up", 22, 4, w=w_up, w0=0, norm=2, layer=0)
    DOWN0 = Phase("fin", 4, 11, w=w_down, w0=0, norm=0, gain=GAIN_KV)
    KEY = Phase("scale", 4, 4, w=w_k, w0=0, norm=3)
    VAL = Phase("scale", 4, 4, w=w_v, w0=0, norm=0)
    QRY = Phase("scale", 4, 4, w=w_q, w0=0, norm=0)
    WO = Phase("fin", 4, 4, w=w_o, w0=0, norm=0, gain=GAIN_FFN1)
    UP1 = Phase("up", 22, 4, w=w_up, w0=n_ffn_units, norm=4, layer=1)
    DOWN1 = Phase("fin", 4, 11, w=w_down, w0=44, norm=0, gain=GAIN_FINAL)
    PHASES = [WIN, GLU, UP0, DOWN0, KEY, VAL, QRY, WO, UP1, DOWN1]

    with ExitStack() as ctx:
        def sb(name, shape, dt=F32, stack=ctx):
            return stack.enter_context(nc.sbuf_tensor(name, shape, dt))

        def sem(name):
            return ctx.enter_context(nc.semaphore(name))

        acc = ctx.enter_context(nc.psum_tensor("acc", [P, 2, 4, 512], F32))

        x = sb("x", [P, KT, SEQ])
        raw = sb("raw", [P, 2, UNIT_KT, STRIP])
        w_high = sb("w_high", [P, 2, UNIT_KT, STRIP], F32R)
        w_low = sb("w_low", [P, 2, UNIT_KT, STRIP], F32R)
        reduced = sb("reduced", [P, 4, SEQ])
        xg = sb("xg", [P, 4, SEQ])
        square_sum = sb("square_sum", [P, SEQ])
        rstd = sb("rstd", [P, SEQ])
        ones = sb("ones", [P, P])
        ident = sb("ident", [P, P])
        eps = sb("eps", [P, 1])
        g_sb = sb("g_sb", [P, 6, KT])
        conv_sb = sb("conv_sb", [P, 2, CONV_WIDTH + 1, FT])
        d_sb = sb("d_sb", [P, KT])
        a4 = sb("a4", [P, 2, 2, PAIRS])
        wf_sb = sb("wf_sb", [P, KT, HEADS])
        bf_sb = sb("bf_sb", [HEADS, 1])
        with ExitStack() as s:
            square = sb("square", [P, 2, SEQ], F32, s)
            gate = sb("gate", [P, 2, SEQ + 2], F32, s)
            conv_acc = sb("conv_acc", [P, 2, SEQ], F32, s)
            value = sb("value", [P, 2, SEQ], F32, s)
        with ExitStack() as s:
            q_st = sb("q_st", [P, 2, SEQ], F32, s)
            v_st = sb("v_st", [P, 2, SEQ], F32, s)
            ck_st = sb("ck_st", [HEADS, 2, SEQ], F32, s)
            v_tok = sb("v_tok", [P, 2, SEQ], F32, s)
        sb("epilogue_room", [P, 2 * 4 * SEQ + 8])
        with ExitStack() as s:
            st1 = sb("st1", [P, CHUNK, 2, PAIRS], F32, s)
        xs = sb("xs", [P, KT, 2, SEQ], F32R)
        with ExitStack() as s:
            u = sb("u", [P, KT, SEQ], F32, s)
            with ExitStack() as s2:
                b_nat = sb("b_nat", [P, 2, PAIRS, GROUP], F32, s2)
            with ExitStack() as s2:
                bt = sb("bt", [P, KT, 2, P], F32, s2)
                cb = sb("cb", [P, 2, PAIRS, 2, GROUP], F32, s2)
            ys = sb("ys", [P, KT, 2, SEQ], F32R, s)
            with ExitStack() as s2:
                c_nat = sb("c_nat", [P, 2, PAIRS, GROUP], F32, s2)
            dg = sb("dg", [P, KT, P], F32, s)
            with ExitStack() as s2:
                bb = sb("bb", [P, 2, PAIRS, 2, GROUP], F32, s2)
                prod = sb("prod", [P, 2, PAIRS, GROUP], F32, s2)
                scr = sb("scr", [P, 30, PAIRS], F32, s2)
                scr_i = sb("scr_i", [P, PAIRS], I32, s2)
            st0 = sb("st0", [P, CHUNK, 2, PAIRS], F32, s)
        with ExitStack() as s:
            xq = sb("xq", [P, KT, 2, SEQ], F32R, s)
            kT = sb("kT", [P, HEADS, SEQ], F32, s)
            vT = sb("vT", [P, HEADS, SEQ], F32, s)
            qT = sb("qT", [P, HEADS, SEQ], F32, s)
            c16 = sb("c16", [HEADS, 5, SEQ], F32, s)
            mask = sb("mask", [P, 3 * P], F32, s)
        with ExitStack() as s:
            os_ = sb("os", [P, HEADS, 2, SEQ], F32R, s)
        hs = sb("hs", [P, FT, 2, SEQ], F32R)
        pr = reduced[:].rearrange("p b t -> p (b t)")[:, 0:6 * P].rearrange("p (b k) -> p b k", b=2)
        pt = xg[:].rearrange("p b t -> p (b t)")[:, 0:6 * P].rearrange("p (b k) -> p b k", b=2)
        e16 = sb("e16", [HEADS, HEADS])
        cq = sb("cq", [P, 2, HEADS])
        negmax = sb("negmax", [P, 2, 2])
        row_sum = sb("row_sum", [P, 2, 2])
        row_inv = sb("row_inv", [P, 2, 2])

        WIN.src, GLU.src, UP0.src, DOWN0.src = xs, ys, xs, hs
        KEY.src, VAL.src, QRY.src, WO.src, UP1.src, DOWN1.src = xs, xs, xq, os_, xs, hs
        WIN.dst, KEY.dst, VAL.dst, QRY.dst = u, kT, vT, qT
        QRY.mul = SCALE

        x_loaded = [sem(f"x_loaded{c}") for c in range(4)]
        gains_loaded = sem("gains_loaded")
        rates_loaded = sem("rates_loaded")
        params_loaded = sem("params_loaded")
        raw_loaded = [sem("raw_loaded0"), sem("raw_loaded1")]
        w_high_done = sem("w_high_done")
        w_split = sem("w_split")
        weights_used = sem("weights_used")
        strip_reduced = sem("strip_reduced")
        scaled = sem("scaled")
        sigmoid_done = sem("sigmoid_done")
        glu_done = sem("glu_done")
        x_updated = sem("x_updated")
        gained = sem("gained")
        x_high = sem("x_high")
        x_split = sem("x_split")
        squares_summed = sem("squares_summed")
        norm_summed = sem("norm_summed")
        root_done = sem("root_done")
        rstd_done = sem("rstd_done")
        gate_scaled = sem("gate_scaled")
        value_scaled = sem("value_scaled")
        conv_started = sem("conv_started")
        conv_done = sem("conv_done")
        gelu_done = sem("gelu_done")
        hidden_ready = sem("hidden_ready")
        hidden_high = sem("hidden_high")
        hidden_split = sem("hidden_split")
        consts_done = sem("consts_done")
        dve_chain = sem("dve_chain")
        pool_chain = sem("pool_chain")
        angle_ready = sem("angle_ready")
        trig_done = sem("trig_done")
        disc_ready = sem("disc_ready")
        disc_taken = sem("disc_taken")
        coef_ready = sem("coef_ready")
        b_bar_ready = sem("b_bar_ready")
        s5_mats_ready = sem("s5_mats_ready")
        s5_filled = sem("s5_filled")
        s5_evacuated = sem("s5_evacuated")
        scan_step = sem("scan_step")
        scanned = sem("scanned")
        y_high = sem("y_high")
        y_split = sem("y_split")
        xq_gained = sem("xq_gained")
        xq_high = sem("xq_high")
        xq_split = sem("xq_split")
        gate_logits = sem("gate_logits")
        gate_taken = sem("gate_taken")
        abs_ready = sem("abs_ready")
        soft_done = sem("soft_done")
        c_ready = sem("c_ready")
        masks_ready = sem("masks_ready")
        cq_turned = sem("cq_turned")
        cq_taken = sem("cq_taken")
        head_staged = sem("head_staged")
        scores_done = sem("scores_done")
        v_turned = sem("v_turned")
        v_taken = sem("v_taken")
        max_done = sem("max_done")
        exp_done = sem("exp_done")
        probs_ready = sem("probs_ready")
        probs_turned = sem("probs_turned")
        probs_taken = sem("probs_taken")
        o_done = sem("o_done")
        o_high = sem("o_high")
        o_split = sem("o_split")
        out_ready = sem("out_ready")
        stored = sem("stored")

        def reach(eng, s, count):
            if isinstance(count, int) and count <= 0:
                return
            eng.wait_ge(s, count)

        def pairs_of_strips(eng, ph, body, chain=None, per=0, peel=1):
            for s in range(2 * peel):
                body(s, s % 2)
            rest = ph.strips // 2 - peel
            if rest == 1:
                body(2 * peel, 0)
                body(2 * peel + 1, 1)
            elif rest > 1:
                with eng.Fori(0, rest) as i:
                    if chain:
                        chain.enter(i, per)
                    body(i * 2 + 2 * peel, 0)
                    body(i * 2 + 2 * peel + 1, 1)
                if chain:
                    chain.leave(rest, per)

        def units_through(ph, s):
            return HALVES * RING + (ph.unit0 + ph.kc) * HALVES + s * (ph.kc * HALVES)

        def half_unit(ph, s, c, h):
            return (ph.unit0 + c) * HALVES + h + s * (ph.kc * HALVES)

        def half_tiles(h):
            return slice(h * UNIT_KT // HALVES, (h + 1) * UNIT_KT // HALVES)

        def reduced_free(eng, ph, s):
            if isinstance(s, int) and s == 0:
                at = PHASES.index(ph)
                if at == 0:
                    return
                ph, s = PHASES[at - 1], PHASES[at - 1].strips
            if ph.kind == "scale":
                reach(eng, scaled, ph.scale0 + s)
            elif ph.kind == "up":
                reach(eng, gate_scaled, ph.up0 + s)
                reach(eng, value_scaled, ph.up0 + s)
            else:
                reach(eng, x_updated, ph.fin0 + s)

        block = ctx.enter_context(nc.Block())

        @block.sync
        def _(sp):
            for c in range(4):
                sp.dma_start(x[:, 4 * c:4 * c + 4], xT[:, 4 * c:4 * c + 4]).then_inc(x_loaded[c], 16)
            for ph in PHASES:
                with sp.Fori(0, ph.strips * ph.kc // 2) as i:
                    for slot in range(2):
                        sp.wait_ge(w_split, i * (2 * HALVES) + (ph.unit0 + slot + 1) * HALVES)
                        sp.dma_start(raw[:, slot].rearrange("p k n -> p (k n)"),
                                     ph.w[bass.ds(i * 2 + (ph.w0 + slot), 1)].rearrange("o p n -> (o p) n")
                                     ).then_inc(raw_loaded[slot], 16)
            for c in range(4):
                sp.wait_ge(out_ready, c + 1)
                sp.dma_start(out[:, 4 * c:4 * c + 4], x[:, 4 * c:4 * c + 4]).then_inc(stored, 16)
            sp.wait_ge(stored, 64)

        @block.tensor
        def _(pe):
            pe.sem_inc(weights_used, RING * HALVES)
            pe.wait_ge(consts_done, 2)

            def unit(ph, s, par, c, last_bank_wait=None):
                slot = (par * ph.kc + c) % 2
                for k in range(UNIT_KT):
                    if k % (UNIT_KT // HALVES) == 0:
                        pe.wait_ge(w_split, half_unit(ph, s, c, k * HALVES // UNIT_KT) + RING * HALVES + 1)
                    for m in range(4):
                        if last_bank_wait and c == 0 and k == 0 and m == 3:
                            pe.wait_ge(*last_bank_wait)
                        kt = c * UNIT_KT + k
                        cols = slice(m * P, (m + 1) * P)
                        first, last = kt == 0, kt == ph.kc * UNIT_KT - 1
                        pe.matmul(acc[:, par, m, :], w_high[:, slot, k, cols],
                                  ph.src[:, kt].rearrange("p h t -> p (h t)"),
                                  start=first, stop=last, skip_group_check=True)
                        mm = pe.matmul(acc[:, par, m, 0:SEQ], w_low[:, slot, k, cols],
                                       ph.src[:, kt, 0], start=False, stop=last,
                                       skip_group_check=True)
                    if (k + 1) % (UNIT_KT // HALVES) == 0:
                        mm.then_inc(weights_used, 1)

            def input_ready(ph, c):
                if ph is WIN:
                    pe.wait_ge(x_split, c + 1)
                elif ph is GLU:
                    pe.wait_ge(y_split, c + 1)
                elif ph is UP0 or ph is UP1:
                    before = GLU if ph is UP0 else WO
                    per = before.strips // 4
                    pe.wait_ge(x_split, before.fin0 + per * (c + 1))
                elif ph is DOWN0 or ph is DOWN1:
                    before = UP0 if ph is DOWN0 else UP1
                    pe.wait_ge(hidden_split, before.up0 + 2 * (c + 1))
                elif ph is KEY:
                    pe.wait_ge(x_split, DOWN0.fin0 + c + 1)
                elif ph is QRY:
                    pe.wait_ge(xq_split, c + 1)
                elif ph is WO:
                    pe.wait_ge(o_split, 4 * c + 4 + 2)

            def phase(ph):
                def strip(s, par, first=False, wait3=None):
                    pe.wait_ge(strip_reduced, ph.strip0 + s + 1)
                    for c in range(ph.kc):
                        if first:
                            input_ready(ph, c)
                        unit(ph, s, par, c, wait3)

                strip(0, 0, True)
                if ph.norm:
                    pe.wait_ge(strip_reduced, ph.strip0 + 2)
                    fin_before = {1: 4, 2: GLU.fin0 + 8, 3: DOWN0.fin0 + 4, 4: WO.fin0 + 4}[ph.norm]
                    pe.wait_ge(squares_summed, fin_before)
                    pe.matmul(acc[:, 1, 3, 0:SEQ], ones[:], square_sum[:], start=True, stop=True
                              ).then_inc(norm_summed, 1)
                    strip(1, 1, False, (root_done, ph.norm))
                else:
                    strip(1, 1)
                rest = ph.strips // 2 - 1
                if rest == 1:
                    strip(2, 0)
                    strip(3, 1)
                else:
                    with pe.Fori(0, rest) as i:
                        strip(i * 2 + 2, 0)
                        strip(i * 2 + 3, 1)

            def s5():
                fills = [0]

                def begin():
                    k = fills[0]
                    if k < 2:
                        pe.wait_ge(strip_reduced, WIN.strips + 1 + k)
                    else:
                        pe.wait_ge(s5_evacuated, k - 1)
                    fills[0] += 1
                    return k % 2

                pe.wait_ge(b_bar_ready, 1)
                for f in range(2):
                    par = begin()
                    for j in range(16):
                        mt, ri = (f * 16 + j) // 2, j % 2
                        ins = pe.transpose(acc[:, par, j // 4, (j % 4) * P:(j % 4 + 1) * P],
                                           bb[:, ri, 4 * mt:4 * mt + 4].rearrange("p q g c -> p (q g c)"),
                                           ident[:])
                    ins.then_inc(s5_filled, 1)

                def inputs(c):
                    tok = slice(c * CHUNK, (c + 1) * CHUNK)
                    for grp in range(4):
                        par = begin()
                        for m in range(4):
                            mt = grp * 4 + m
                            for ri in range(2):
                                for j in range(4):
                                    rows = slice(32 * j, 32 * j + 32)
                                    col = (m * 2 + ri) * CHUNK
                                    ins = pe.matmul(acc[:, par, j, col:col + CHUNK],
                                                    bt[rows, mt, ri, :], u[rows, mt, tok],
                                                    start=True, stop=True)
                        ins.then_inc(s5_filled, 1)

                def outputs(c):
                    tok = slice(c * CHUNK, (c + 1) * CHUNK)
                    st = (st0, st1)[c % 2]
                    par = begin()
                    pe.wait_ge(scanned, c + 1)
                    for mt in range(KT):
                        cols = slice((mt % 8) * CHUNK, (mt % 8 + 1) * CHUNK)
                        pe.matmul(acc[:, par, mt // 8, cols], dg[:, mt, :], u[:, mt, tok],
                                  start=True, stop=False, skip_group_check=True)
                        for j in range(4):
                            for ri in range(2):
                                ins = pe.matmul(acc[32 * j:32 * j + 32, par, mt // 8, cols],
                                                cb[:, ri, 4 * mt + j].rearrange("p g c -> p (g c)"),
                                                st[:, :, ri, 4 * mt + j], start=False,
                                                stop=(ri == 1), skip_group_check=True)
                    ins.then_inc(s5_filled, 1)

                pe.wait_ge(s5_evacuated, 2)
                pe.wait_ge(scaled, WIN.strips)
                inputs(0)
                inputs(1)
                pe.wait_ge(s5_mats_ready, 2)
                outputs(0)
                for c in range(2, CHUNKS):
                    inputs(c)
                    outputs(c - 1)
                outputs(CHUNKS - 1)
                pe.wait_ge(s5_evacuated, fills[0])

            def forget_gate():
                pe.wait_ge(params_loaded, 16 * 6)
                pe.wait_ge(strip_reduced, VAL.strip0 + VAL.strips + 1)
                for kt in range(KT):
                    ins = pe.matmul(acc[0:HEADS, 0, 0, :], wf_sb[:, kt, :],
                                    xs[:, kt].rearrange("p h t -> p (h t)").bitcast(F32),
                                    start=(kt == 0), stop=(kt == KT - 1))
                ins.then_inc(gate_logits, 1)
                pe.wait_ge(gate_taken, 1)

            def attention():
                pe.wait_ge(strip_reduced, QRY.strip0 + QRY.strips + 2)
                pe.wait_ge(c_ready, 1)
                for qb in range(2):
                    ins = pe.transpose(acc[:, 0, 0, qb * HEADS:(qb + 1) * HEADS],
                                       c16[:, 1, qb * P:(qb + 1) * P], ident[0:HEADS, 0:HEADS])
                ins.then_inc(cq_turned, 1)
                pe.wait_ge(cq_taken, 1)

                def scores(h, b):
                    pe.wait_ge(head_staged, h + 1)
                    if not isinstance(h, int) or h >= 2:
                        pe.wait_ge(max_done, h - 1)
                        pe.wait_ge(v_taken, h - 1)
                    s_bank = acc[:, b, 0]
                    pe.matmul(s_bank[:, 0:P], q_st[:, b, 0:P], kT[:, bass.ds(h, 1), 0:P].rearrange("p o t -> p (o t)"),
                              start=True, stop=False)
                    pe.matmul(s_bank[:, 0:P], ones[0:HEADS, :], ck_st[:, b, 0:P], start=False, stop=True)
                    pe.matmul(s_bank[:, P:3 * P], q_st[:, b, P:2 * P],
                              kT[:, bass.ds(h, 1), :].rearrange("p o t -> p (o t)"), start=True, stop=False)
                    pe.matmul(s_bank[:, P:3 * P], ones[0:HEADS, :], ck_st[:, b, :], start=False, stop=True
                              ).then_inc(scores_done, 1)
                    pe.transpose(acc[:, b, 1, 0:P], v_st[:, b, 0:P], ident[:])
                    pe.transpose(acc[:, b, 1, P:2 * P], v_st[:, b, P:2 * P], ident[:]).then_inc(v_turned, 1)

                def turn(h, b):
                    pe.wait_ge(probs_ready, h + 1)
                    pe.wait_ge(probs_taken, h + 1)
                    for j in range(3):
                        ins = pe.transpose(acc[:, b, 2, j * P:(j + 1) * P], pr[:, b, j * P:(j + 1) * P], ident[:])
                    ins.then_inc(probs_turned, 1)

                def mix(h, b):
                    pe.wait_ge(probs_taken, h + 3)
                    pe.wait_ge(v_taken, h + 1)
                    pe.wait_ge(o_split, h + 1)
                    pe.matmul(acc[:, b, 3, 0:SEQ], v_tok[:, b, 0:P], pt[:, b, 0:SEQ], start=True, stop=False,
                              skip_group_check=True)
                    pe.matmul(acc[:, b, 3, P:SEQ], v_tok[:, b, P:SEQ], pt[:, b, SEQ:3 * P], start=False,
                              stop=True, skip_group_check=True).then_inc(o_done, 1)

                scores(0, 0)
                scores(1, 1)
                turn(0, 0)
                with pe.Fori(0, HEADS // 2 - 1) as i:
                    for b in range(2):
                        scores(i * 2 + (b + 2), b)
                        turn(i * 2 + (b + 1), 1 - b)
                        mix(i * 2 + b, b)
                turn(HEADS - 1, 1)
                mix(HEADS - 2, 0)
                mix(HEADS - 1, 1)
                pe.wait_ge(o_split, HEADS + 2)

            phase(WIN)
            s5()
            phase(GLU)
            phase(UP0)
            phase(DOWN0)
            phase(KEY)
            phase(VAL)
            forget_gate()
            phase(QRY)
            attention()
            phase(WO)
            phase(UP1)
            phase(DOWN1)
            pe.wait_ge(squares_summed, DOWN1.fin0 + DOWN1.strips)
            pe.wait_ge(strip_reduced, DOWN1.strip0 + DOWN1.strips + 2)
            pe.matmul(acc[:, 1, 3, 0:SEQ], ones[:], square_sum[:], start=True, stop=True).then_inc(norm_summed, 1)

        @block.scalar
        def _(act):
            act.dma_start(g_sb[:], gains).then_inc(gains_loaded, 16)
            for ri in range(2):
                act.dma_start(scr[:, ri], lam[:, ri]).then_inc(rates_loaded, 16)
            for g2 in range(2):
                act.dma_start(scr[64 * g2:64 * g2 + 64, 2],
                              log_step[g2:g2 + 1, :].to_broadcast([64, PAIRS])).then_inc(rates_loaded, 16)
            for dst, src in ((b_nat, b_in), (c_nat, c_out), (conv_sb, conv), (d_sb, skip_d), (wf_sb, w_f),
                             (bf_sb, b_f)):
                act.dma_start(dst[:], src).then_inc(params_loaded, 16)

            def high(ph, s, par, c):
                slot = (par * ph.kc + c) % 2
                act.wait_ge(raw_loaded[slot], loads(ph, s, par, c))
                for h in range(HALVES):
                    act.wait_ge(weights_used, half_unit(ph, s, c, h) + 1)
                    act.activation(w_high[:, slot, half_tiles(h)], raw[:, slot, half_tiles(h)], ACT.Copy
                                   ).then_inc(w_high_done, 1)

            def loads(ph, s, par, c):
                return (s - par) * (8 * ph.kc) + 16 * ((ph.unit0 + par * ph.kc + c) // 2 + 1)

            def rms_root(n):
                act.wait_ge(norm_summed, n)
                act.activation(rstd[:], acc[:, 1, 3, 0:SEQ], ACT.Sqrt, bias=eps[:], scale=1.0 / D_MODEL
                               ).then_inc(root_done, 1)

            def fin_high(n, tile, nt):
                act.wait_ge(gained, n + 1)
                act.activation(xs[:, bass.ds(tile, nt), 0, :], xg[:, 0:nt], ACT.Copy).then_inc(x_high, 1)

            def epilogue(ph, s, slot):
                if ph.kind == "glu":
                    if slot == 0:
                        act.wait_ge(strip_reduced, ph.strip0 + s + 3)
                        act.activation(value[:], reduced[:, 2:4], ACT.Sigmoid).then_inc(sigmoid_done, 1)
                    if slot == 2:
                        fin_high(ph.fin0 + s, s * 2, 2)
                elif ph.kind == "fin":
                    if slot == 1 and ph is not DOWN1:
                        fin_high(ph.fin0 + s, s * 4, 4)
                elif ph.kind == "up":
                    n = ph.up0 + s
                    if slot == 0:
                        act.wait_ge(gate_scaled, n + 1)
                        reach(act, hidden_ready, n)
                        for j in range(2):
                            ins = act.activation(conv_acc[:, j], gate[:, j, 2:SEQ + 2], ACT.Identity,
                                                 bias=conv_sb[:, ph.layer, 3, bass.ds(s * 2 + j, 1)],
                                                 scale=conv_sb[:, ph.layer, 2, bass.ds(s * 2 + j, 1)])
                        ins.then_inc(conv_started, 1)
                    if slot == 2:
                        act.wait_ge(conv_done, n + 1)
                        act.activation(conv_acc[:], conv_acc[:], ACT.Gelu_apprx_tanh).then_inc(gelu_done, 1)
                        act.wait_ge(hidden_ready, n + 1)
                        act.activation(hs[:, bass.ds(s * 2, 2), 0, :], value[:], ACT.Copy
                                       ).then_inc(hidden_high, 1)

            def phase(ph, before):
                def strip(s, par, prev):
                    for c in range(ph.kc):
                        if ph.norm and isinstance(s, int) and s == 1 and c == 1:
                            rms_root(ph.norm)
                        high(ph, s, par, c)
                        if 1 <= c <= 3:
                            prev(c - 1)

                def body(s, par):
                    first = isinstance(s, int) and s == 0
                    strip(s, par, before if first else (lambda slot: epilogue(ph, s - 1, slot)))

                pairs_of_strips(act, ph, body)
                return lambda slot: epilogue(ph, ph.strips - 1, slot)

            def s5():
                for f in range(2):
                    act.wait_ge(s5_filled, f + 1)
                    for bank in range(4):
                        mt = f * 8 + bank * 2
                        ins = act.activation(bt[:, mt:mt + 2].rearrange("p m r s -> p (m r s)"),
                                             acc[:, f % 2, bank], ACT.Copy)
                    ins.then_inc(s5_evacuated, 1)
                fills = [2]

                def inputs(c):
                    st = (st0, st1)[c % 2]
                    for grp in range(4):
                        par = fills[0] % 2
                        fills[0] += 1
                        act.wait_ge(s5_filled, fills[0])
                        for j in range(4):
                            q0 = grp * 16 + j
                            dst = st[:, :, :, q0:q0 + 13:4].rearrange("p t r m -> p m r t")
                            ins = act.activation(dst, acc[:, par, j].rearrange(
                                "p (m r t) -> p m r t", m=4, r=2), ACT.Copy)
                        ins.then_inc(s5_evacuated, 1)

                def outputs(c):
                    par = fills[0] % 2
                    fills[0] += 1
                    act.wait_ge(s5_filled, fills[0])
                    for half in range(2):
                        ins = act.activation(u[:, 8 * half:8 * half + 8, c * CHUNK:(c + 1) * CHUNK],
                                             acc[:, par, half].rearrange("p (m t) -> p m t", m=8),
                                             ACT.Gelu_apprx_tanh)
                    ins.then_inc(s5_evacuated, 1)

                inputs(0)
                inputs(1)
                outputs(0)
                for c in range(2, CHUNKS):
                    inputs(c)
                    outputs(c - 1)
                outputs(CHUNKS - 1)
                act.wait_ge(s5_evacuated, fills[0])
                for c in range(4):
                    act.activation(ys[:, 4 * c:4 * c + 4, 0, :], u[:, 4 * c:4 * c + 4], ACT.Copy
                                   ).then_inc(y_high, 1)

            def log_sigmoid():
                act.wait_ge(abs_ready, 1)
                act.activation(c16[:, 2], c16[:, 3], ACT.Exp, scale=-1.0).then_inc(soft_done, 1)
                act.wait_ge(abs_ready, 2)
                act.activation(c16[:, 3], c16[:, 4], ACT.Ln).then_inc(soft_done, 1)

            def attention():
                act.wait_ge(cq_turned, 1)
                act.activation(cq[:], acc[:, 0, 0, 0:2 * HEADS].rearrange("p (b h) -> p b h", b=2), ACT.Copy
                               ).then_inc(cq_taken, 1)

                def exps(h, b):
                    act.wait_ge(max_done, h + 1)
                    for j, cols in ((0, slice(0, P)), (1, slice(P, 3 * P))):
                        ins = act.activation(pr[:, b, cols], pr[:, b, cols], ACT.Exp, bias=negmax[:, b, j:j + 1],
                                             accum_out=row_sum[:, b, j:j + 1])
                    ins.then_inc(exp_done, 1)

                def take_v(h, b):
                    act.wait_ge(v_turned, h + 1)
                    act.wait_ge(o_done, h + 1)
                    act.activation(v_tok[:, b], acc[:, b, 1, 0:SEQ], ACT.Copy).then_inc(v_taken, 1)

                def take_probs(h, b):
                    act.wait_ge(probs_turned, h + 1)
                    act.wait_ge(o_done, h + 1)
                    act.activation(pt[:, b], acc[:, b, 2, 0:3 * P], ACT.Copy).then_inc(probs_taken, 1)

                def take_o(h, b):
                    act.wait_ge(o_done, h + 3)
                    act.activation(os_[:, bass.ds(h, 1), 0, :].rearrange("p o t -> p (o t)"),
                                   acc[:, b, 3, 0:SEQ], ACT.Copy).then_inc(o_high, 1)

                exps(0, 0)
                take_v(0, 0)
                exps(1, 1)
                take_probs(0, 0)
                take_v(1, 1)
                with act.Fori(0, HEADS // 2 - 1) as i:
                    for b in range(2):
                        exps(i * 2 + (b + 2), b)
                        take_probs(i * 2 + (b + 1), 1 - b)
                        take_o(i * 2 + b, b)
                        take_v(i * 2 + (b + 2), b)
                take_probs(HEADS - 1, 1)
                take_o(HEADS - 2, 0)
                take_o(HEADS - 1, 1)

            act.wait_ge(consts_done, 2)
            fin_high(0, 0, 4)
            fin_high(1, 4, 4)

            def bring_in(slot):
                if slot < 2:
                    fin_high(2 + slot, 8 + 4 * slot, 4)
                else:
                    act.wait_ge(angle_ready, 1)
                    act.activation(scr[:, 8], scr[:, 7], ACT.Sin)
                    act.activation(scr[:, 10], scr[:, 9], ACT.Sin).then_inc(trig_done, 1)

            prev = phase(WIN, bring_in)

            def after_win(slot, prev=prev):
                prev(slot)
                if slot == 0:
                    s5()

            prev = phase(GLU, after_win)
            prev = phase(UP0, prev)
            prev = phase(DOWN0, prev)
            prev = phase(KEY, prev)

            def after_key(slot, prev=prev):
                prev(slot)
                act.wait_ge(xq_gained, slot + 1)
                act.activation(xq[:, 4 * slot:4 * slot + 4, 0, :], xg[:], ACT.Copy).then_inc(xq_high, 1)
                if slot == 2:
                    act.wait_ge(xq_gained, 4)
                    act.activation(xq[:, 12:16, 0, :], xg[:], ACT.Copy).then_inc(xq_high, 1)

            prev = phase(VAL, after_key)

            def after_value(slot, prev=prev):
                prev(slot)
                if slot == 0:
                    log_sigmoid()

            prev = phase(QRY, after_value)

            def after_query(slot, prev=prev):
                prev(slot)
                if slot == 0:
                    attention()

            prev = phase(WO, after_query)
            prev = phase(UP1, prev)
            prev = phase(DOWN1, prev)
            rms_root(5)

        @block.vector
        def _(dve):
            dve.sem_inc(w_split, RING * HALVES)
            dve.sem_inc(strip_reduced, 2)
            dve.sem_inc(scan_step, 2)
            dve.sem_inc(o_split, 2)
            dve.sem_inc(probs_taken, 2)
            dve.sem_inc(o_done, 2)
            dve.sem_inc(x_updated, 4)
            chain = Chain(dve, dve_chain)

            def low(ph, s, par, c):
                slot = (par * ph.kc + c) % 2
                for h in range(HALVES):
                    dve.wait_ge(w_high_done, half_unit(ph, s, c, h) + 1)
                    tiles = half_tiles(h)
                    dve.tensor_tensor(w_low[:, slot, tiles], raw[:, slot, tiles],
                                      w_high[:, slot, tiles].bitcast(F32), ALU.subtract).then_inc(w_split, 1)

            def rms_inverse(n):
                dve.wait_ge(root_done, n)
                dve.reciprocal(rstd[:], rstd[:]).then_inc(rstd_done, 1)
                dve.wait_ge(rstd_done, n)

            def all_rows(ap, k):
                return ap.unsqueeze(1).to_broadcast([P, k, SEQ])

            def reduce_strip(ph, s, par):
                dve.wait_ge(weights_used, units_through(ph, s))
                reduced_free(dve, ph, s)
                dve.tensor_reduce(reduced[:], acc[:, par].rearrange("p b (h t) -> p b t h", h=2), AX_X, ALU.add
                                  ).then_inc(strip_reduced, 1)
                dve.wait_ge(strip_reduced, ph.strip0 + s + 3)

            def gain(n, tile, nt, which):
                if n is not None:
                    dve.wait_ge(x_updated, n + 1)
                for j in range(nt):
                    ins = dve.tensor_scalar(xg[:, j], x[:, bass.ds(tile + j, 1)].rearrange("p o t -> p (o t)"),
                                            g_sb[:, which, bass.ds(tile + j, 1)], None, ALU.mult)
                return ins

            def fin_low(n, tile, nt):
                dve.wait_ge(x_high, n + 1)
                dve.tensor_tensor(xs[:, bass.ds(tile, nt), 1, :], xg[:, 0:nt],
                                  xs[:, bass.ds(tile, nt), 0, :].bitcast(F32), ALU.subtract).then_inc(x_split, 1)

            def epilogue(ph, s, par, slot):
                if ph.kind == "scale" and slot == 0:
                    reduce_strip(ph, s, par)
                    dst = ph.dst[:, bass.ds(s * 4, 4)]
                    if ph.mul == 1.0:
                        ins = dve.tensor_tensor(dst, reduced[:], all_rows(rstd[:], 4), ALU.mult)
                    else:
                        ins = dve.scalar_tensor_tensor(dst, reduced[:], ph.mul, all_rows(rstd[:], 4),
                                                       ALU.mult, ALU.mult)
                    ins.then_inc(scaled, 1)
                elif ph.kind == "glu":
                    n = ph.fin0 + s
                    if slot == 0:
                        reduce_strip(ph, s, par)
                    if slot == 1:
                        dve.wait_ge(sigmoid_done, s + 1)
                        dve.tensor_tensor(reduced[:, 0:2], reduced[:, 0:2], value[:], ALU.mult).then_inc(glu_done, 1)
                        dve.wait_ge(glu_done, s + 1)
                        tiles = x[:, bass.ds(s * 2, 2)]
                        dve.tensor_tensor(tiles, tiles, reduced[:, 0:2], ALU.add).then_inc(x_updated, 1)
                        dve.wait_ge(x_split, n)
                        gain(n, s * 2, 2, ph.gain).then_inc(gained, 1)
                    if slot == 2:
                        fin_low(n, s * 2, 2)
                elif ph.kind == "fin":
                    n = ph.fin0 + s
                    if slot == 0:
                        reduce_strip(ph, s, par)
                        tiles = x[:, bass.ds(s * 4, 4)]
                        dve.tensor_tensor(tiles, tiles, reduced[:], ALU.add).then_inc(x_updated, 1)
                        if ph is not DOWN1:
                            dve.wait_ge(x_split, n)
                            gain(n, s * 4, 4, ph.gain).then_inc(gained, 1)
                    if slot == 2 and ph is not DOWN1:
                        fin_low(n, s * 4, 4)
                elif ph.kind == "up":
                    n = ph.up0 + s
                    if slot == 0:
                        reduce_strip(ph, s, par)
                        reach(dve, conv_done, n)
                        dve.tensor_tensor(gate[:, :, 2:SEQ + 2], reduced[:, 0:2], all_rows(rstd[:], 2), ALU.mult
                                          ).then_inc(gate_scaled, 1)
                    if slot == 1:
                        dve.wait_ge(conv_started, n + 1)
                        for tap, order in ((1, 0), (0, 1)):
                            for j in range(2):
                                ins = dve.scalar_tensor_tensor(
                                    conv_acc[:, j], gate[:, j, tap:tap + SEQ],
                                    conv_sb[:, ph.layer, tap, bass.ds(s * 2 + j, 1)], conv_acc[:, j],
                                    ALU.mult, ALU.add)
                                if tap == 1:
                                    chain.step(ins)
                            if tap == 1:
                                chain.wait()
                        ins.then_inc(conv_done, 1)

            def phase(ph, before):
                def strip(s, par, prev):
                    for c in range(ph.kc):
                        low(ph, s, par, c)
                        if 1 <= c <= 3:
                            if c == 1 and ph.norm and isinstance(s, int) and s == 1:
                                rms_inverse(ph.norm)
                            prev(c - 1)

                def body(s, par):
                    first = isinstance(s, int) and s == 0
                    strip(s, par, before if first else (lambda slot: epilogue(ph, s - 1, 1 - par, slot)))

                pairs_of_strips(dve, ph, body, chain, 4 if ph.kind == "up" else 0)
                return lambda slot: epilogue(ph, ph.strips - 1, 1, slot)

            def s5():
                ops = [0]

                def op(out_ap, a, b, alu):
                    dve.wait_ge(scan_step, base[0] + ops[0] + 1)
                    dve.tensor_tensor(out_ap, a, b, alu).then_inc(scan_step, 1)
                    ops[0] += 1

                base = [0]
                p4, t2 = reduced, xg
                half = PAIRS // 2
                p4v = p4[:, 0:2].rearrange("p h (o i q) -> p h o i q", o=2, i=2)[:, :, :, :, 0:half]
                t2v = t2[:, 0, 0:2 * PAIRS].rearrange("p (h o q) -> p h o q", h=2, o=2)

                def step(prev, cur):
                    hs_ = [slice(0, half), slice(half, PAIRS)]
                    for h in range(2):
                        op(p4v[:, h], a4[:, :, :, hs_[h]],
                           prev[:, :, hs_[h]].unsqueeze(1).to_broadcast([P, 2, 2, half]), ALU.mult)
                    for h in range(2):
                        op(t2v[:, h], p4v[:, h, :, 0], p4v[:, h, :, 1], ALU.add)
                    for h in range(2):
                        op(cur[:, :, hs_[h]], cur[:, :, hs_[h]], t2v[:, h], ALU.add)

                def at(st, t):
                    return st[:, bass.ds(t, 1)].rearrange("p o r q -> p (o r) q")

                carry = xg[:, 1, 0:2 * PAIRS].rearrange("p (o q) -> p o q", o=2)
                UNROLL = 7
                for c in range(CHUNKS):
                    st = (st0, st1)[c % 2]
                    through = 2 + 4 * (c + 1) + max(0, c - 1)
                    dve.wait_ge(s5_evacuated, through)
                    if c == 0:
                        dve.wait_ge(disc_taken, 1)
                    else:
                        dve.wait_ge(scanned, c)
                        step(carry, at(st, 0))
                    start = base[0] + ops[0]
                    with dve.Fori(0, (CHUNK - 1) // UNROLL) as i:
                        base[0], ops[0] = start + i * (6 * UNROLL), 0
                        for k in range(UNROLL):
                            step(at(st, i * UNROLL + k), at(st, i * UNROLL + (k + 1)))
                    base[0], ops[0] = start + 6 * (CHUNK - 1), 0
                    dve.wait_ge(scan_step, base[0] + 2)
                    dve.tensor_copy(carry, st[:, CHUNK - 1]).then_inc(scanned, 1)
                for c in range(4):
                    dve.wait_ge(y_high, c + 1)
                    dve.tensor_tensor(ys[:, 4 * c:4 * c + 4, 1, :], u[:, 4 * c:4 * c + 4],
                                      ys[:, 4 * c:4 * c + 4, 0, :].bitcast(F32), ALU.subtract).then_inc(y_split, 1)

            def forget_gate():
                dve.wait_ge(gate_logits, 1)
                chain.step(dve.tensor_reduce(c16[:, 0], acc[0:HEADS, 0, 0].rearrange("p (h t) -> p t h", h=2),
                                             AX_X, ALU.add))
                chain.wait()
                dve.tensor_tensor(c16[:, 1], c16[:, 0], rstd[0:HEADS], ALU.mult).then_inc(gate_taken, 1)
                dve.wait_ge(gate_taken, 1)
                chain.step(dve.tensor_scalar(c16[:, 0], c16[:, 1], bf_sb[:], None, ALU.add))
                chain.wait()
                dve.scalar_tensor_tensor(c16[:, 3], c16[:, 0], -1.0, c16[:, 0], ALU.mult, ALU.max).then_inc(abs_ready, 1)
                dve.wait_ge(soft_done, 1)
                dve.tensor_scalar(c16[:, 4], c16[:, 2], 1.0, None, ALU.add).then_inc(abs_ready, 1)
                dve.wait_ge(abs_ready, 2)
                chain.step(dve.tensor_scalar(c16[:, 1], c16[:, 4], -1.0, 2.0 ** -24, ALU.add, ALU.max))
                chain.wait()
                dve.wait_ge(soft_done, 2)
                chain.step(dve.reciprocal(c16[:, 4], c16[:, 1]))
                chain.wait()
                chain.step(dve.tensor_tensor(c16[:, 1], c16[:, 2], c16[:, 4], ALU.mult))
                chain.wait()
                chain.step(dve.tensor_tensor(c16[:, 2], c16[:, 1], c16[:, 3], ALU.mult))
                chain.wait()
                chain.step(dve.tensor_scalar(c16[:, 3], c16[:, 0], 0.0, None, ALU.min))
                chain.wait()
                chain.step(dve.tensor_tensor(c16[:, 4], c16[:, 3], c16[:, 2], ALU.subtract))
                chain.step(dve.memset(c16[:, 0], 0.0))
                chain.wait()
                chain.step(dve.tensor_scalar(c16[:, 2], c16[:, 0], 1.0, None, ALU.add))
                chain.wait()
                chain.step(dve.tensor_tensor_scan(c16[:, 1], c16[:, 2], c16[:, 4], 0.0, ALU.mult, ALU.add))
                chain.wait()
                dve.tensor_scalar(c16[:, 0], c16[:, 1], -1.0, None, ALU.mult).then_inc(c_ready, 1)

            def attention():
                dve.wait_ge(cq_taken, 1)
                dve.wait_ge(masks_ready, 1)

                def front(h, b):
                    dve.wait_ge(scores_done, h + 1)
                    if not isinstance(h, int) or h >= 2:
                        dve.wait_ge(probs_turned, h - 1)
                    for qb, cols in ((0, slice(0, P)), (1, slice(P, 3 * P))):
                        chain.step(dve.scalar_tensor_tensor(
                            pr[:, b, cols], acc[:, b, 0, cols], cq[:, qb, bass.ds(h, 1)], mask[:, cols],
                            ALU.add, ALU.add))
                    chain.wait()
                    for qb, cols in ((0, slice(0, P)), (1, slice(P, 3 * P))):
                        ins = dve.tensor_reduce(negmax[:, b, qb:qb + 1], pr[:, b, cols], AX_X, ALU.max, negate=True)
                    ins.then_inc(max_done, 1)

                def back(h, b):
                    dve.wait_ge(exp_done, h + 1)
                    chain.step(dve.reciprocal(row_inv[:, b], row_sum[:, b]))
                    chain.wait()
                    for qb, cols in ((0, slice(0, P)), (1, slice(P, 3 * P))):
                        ins = dve.tensor_scalar(pr[:, b, cols], pr[:, b, cols], row_inv[:, b, qb:qb + 1], None,
                                                ALU.mult)
                    ins.then_inc(probs_ready, 1)

                def last(h, b):
                    dve.wait_ge(o_high, h + 1)
                    head = bass.ds(h, 1)
                    dve.tensor_tensor(os_[:, head, 1, :].rearrange("p o t -> p (o t)"), acc[:, b, 3, 0:SEQ],
                                      os_[:, head, 0, :].rearrange("p o t -> p (o t)").bitcast(F32), ALU.subtract
                                      ).then_inc(o_split, 1)

                front(0, 0)
                front(1, 1)
                back(0, 0)
                with dve.Fori(0, HEADS // 2 - 1) as i:
                    chain.enter(i, 6)
                    for b in range(2):
                        back(i * 2 + (b + 1), 1 - b)
                        front(i * 2 + (b + 2), b)
                        last(i * 2 + b, b)
                chain.leave(HEADS // 2 - 1, 6)
                back(HEADS - 1, 1)
                last(HEADS - 2, 0)
                last(HEADS - 1, 1)

            dve.wait_ge(gains_loaded, 16)

            def bring(c):
                dve.wait_ge(x_loaded[c], 16)
                if c:
                    dve.wait_ge(x_split, c)
                gain(None, 4 * c, 4, GAIN_A).then_inc(gained, 1)
                fin_low(c, 4 * c, 4)

            bring(0)
            bring(1)

            def bring_in(slot):
                if slot < 2:
                    bring(2 + slot)
                else:
                    dve.wait_ge(disc_ready, 1)
                    chain.step(dve.tensor_copy(scr_i[:], scr[:, 13]))
                    chain.step(dve.reciprocal(scr[:, 21], scr[:, 20]))
                    chain.wait()
                    dve.tensor_tensor(scr[:, 15], scr[:, 14], scr_i[:].bitcast(F32), ALU.mult
                                      ).then_inc(coef_ready, 1)

            prev = phase(WIN, bring_in)

            def after_win(slot, prev=prev):
                prev(slot)
                if slot == 0:
                    s5()

            prev = phase(GLU, after_win)
            prev = phase(UP0, prev)
            prev = phase(DOWN0, prev)
            prev = phase(KEY, prev)

            def after_key(slot, prev=prev):
                prev(slot)

                def part(c):
                    if c:
                        dve.wait_ge(xq_split, c)
                    else:
                        dve.wait_ge(x_split, DOWN0.fin0 + DOWN0.strips)
                    gain(None, 4 * c, 4, GAIN_B).then_inc(xq_gained, 1)
                    dve.wait_ge(xq_high, c + 1)
                    dve.tensor_tensor(xq[:, 4 * c:4 * c + 4, 1, :], xg[:],
                                      xq[:, 4 * c:4 * c + 4, 0, :].bitcast(F32), ALU.subtract).then_inc(xq_split, 1)

                part(slot)
                if slot == 2:
                    part(3)

            prev = phase(VAL, after_key)

            def after_value(slot, prev=prev):
                prev(slot)
                if slot == 0:
                    forget_gate()

            prev = phase(QRY, after_value)

            def after_query(slot, prev=prev):
                prev(slot)
                if slot == 0:
                    attention()

            prev = phase(WO, after_query)
            prev = phase(UP1, prev)
            prev = phase(DOWN1, prev)
            prev(0)
            rms_inverse(5)
            dve.wait_ge(x_updated, DOWN1.fin0 + DOWN1.strips)
            for c in range(4):
                for j in range(4):
                    kt = 4 * c + j
                    ins = dve.scalar_tensor_tensor(x[:, kt], x[:, kt], g_sb[:, GAIN_FINAL, kt:kt + 1], rstd[:],
                                                   ALU.mult, ALU.mult)
                ins.then_inc(out_ready, 1)

        @block.gpsimd
        def _(pool):
            chain = Chain(pool, pool_chain)

            def do(ins):
                chain.step(ins)
                chain.wait()

            def tt(o, a, b, alu):
                do(pool.tensor_tensor(o, a, b, alu))

            def ts(o, a, s1, op0, s2=None, op1=None):
                do(pool.tensor_scalar(o, a, s1, s2, op0, op1) if op1 else pool.tensor_scalar(o, a, s1, None, op0))

            chain.step(pool.memset(ident[:], 0.0))
            chain.step(pool.memset(eps[:], NORM_EPS))
            chain.step(pool.memset(gate[:, :, 0:2], 0.0))
            chain.wait()
            pool.memset(ones[:], 1.0).then_inc(consts_done, 1)
            pool.affine_select(out=ident[:], in_=ident[:], compare_op=ALU.not_equal, fill=1.0, base=0,
                               pattern=[[-1, P]], channel_multiplier=1).then_inc(consts_done, 1)

            def add_squares(tile, nt):
                for j in range(0, nt, 2):
                    tiles = x[:, bass.ds(tile + j, 2)]
                    tt(square[:], tiles, tiles, ALU.mult)
                    tt(square_sum[:], square_sum[:], square[:, 0], ALU.add)
                    if j == nt - 2:
                        chain.wait()
                        pool.tensor_tensor(square_sum[:], square_sum[:], square[:, 1], ALU.add
                                           ).then_inc(squares_summed, 1)
                    else:
                        tt(square_sum[:], square_sum[:], square[:, 1], ALU.add)

            do(pool.memset(square_sum[:], 0.0))
            for c in range(4):
                pool.wait_ge(x_loaded[c], 16)
                if c:
                    pool.wait_ge(squares_summed, c)
                add_squares(4 * c, 4)

            LR, LI, LS = (scr[:, k] for k in range(3))
            T = [scr[:, k] for k in range(30)]
            pool.wait_ge(rates_loaded, 16 * 4)
            MAGIC = 1.5 * 2.0 ** 23
            LN2_HI, LN2_LO = 0.693359375, -2.12194440e-4
            PI = 3.141592653589793
            TAU_1, TAU_2 = 6.28125, 0.0019350051879882812
            TAU_3 = 2 * PI - TAU_1 - TAU_2

            def exp_poly(o, r, tmp):
                coef = [1 / 5040, 1 / 720, 1 / 120, 1 / 24, 1 / 6, 0.5, 1.0, 1.0]
                ts(o, r, coef[0], ALU.mult, coef[1], ALU.add)
                for a in coef[2:]:
                    tt(tmp, o, r, ALU.mult)
                    ts(o, tmp, a, ALU.add)

            def exp_reduce(o_r, o_k, z, tmp):
                ts(tmp, z, -87.0, ALU.max, 88.0, ALU.min)
                ts(o_k, tmp, 1 / 0.6931471805599453, ALU.mult, MAGIC, ALU.add)
                ts(o_k, o_k, -MAGIC, ALU.add)
                ts(o_r, o_k, -LN2_HI, ALU.mult)
                tt(o_r, o_r, tmp, ALU.add)
                ts(tmp, o_k, -LN2_LO, ALU.mult)
                tt(o_r, o_r, tmp, ALU.add)

            exp_reduce(T[3], T[4], LS, T[5])
            exp_poly(T[6], T[3], T[5])
            ts(T[13], T[4], 127.0, ALU.add, 8388608.0, ALU.mult)
            do(pool.tensor_copy(scr_i[:], T[13]))
            tt(T[11], T[6], scr_i[:].bitcast(F32), ALU.mult)
            tt(T[12], LI, T[11], ALU.mult)
            ts(T[3], T[12], 1 / (2 * PI), ALU.mult, MAGIC, ALU.add)
            ts(T[3], T[3], -MAGIC, ALU.add)
            for tau in (TAU_1, TAU_2, TAU_3):
                ts(T[4], T[3], -tau, ALU.mult)
                tt(T[12], T[12], T[4], ALU.add)
            ts(T[7], T[12], 3.1415925, ALU.min, -3.1415925, ALU.max)
            ts(T[3], T[12], PI / 2, ALU.is_gt)
            ts(T[3], T[3], -2 * PI, ALU.mult, PI / 2, ALU.add)
            tt(T[4], T[12], T[3], ALU.add)
            chain.wait()
            pool.tensor_scalar(T[9], T[4], 3.1415925, -3.1415925, ALU.min, ALU.max).then_inc(angle_ready, 1)
            tt(T[16], LR, T[11], ALU.mult)
            exp_reduce(T[3], T[4], T[16], T[5])
            exp_poly(T[14], T[3], T[5])
            ts(T[13], T[4], 127.0, ALU.add, 8388608.0, ALU.mult)
            tt(T[17], LR, LR, ALU.mult)
            tt(T[18], LI, LI, ALU.mult)
            chain.wait()
            pool.tensor_tensor(T[20], T[17], T[18], ALU.add).then_inc(disc_ready, 1)
            pool.wait_ge(coef_ready, 1)
            pool.wait_ge(trig_done, 1)
            tt(T[22], T[15], T[10], ALU.mult)
            tt(T[23], T[15], T[8], ALU.mult)
            ts(T[24], T[23], -1.0, ALU.mult)
            chain.step(pool.tensor_copy(a4[:, 0, 0], T[22]))
            chain.step(pool.tensor_copy(a4[:, 1, 1], T[22]))
            chain.step(pool.tensor_copy(a4[:, 0, 1], T[24]))
            pool.tensor_copy(a4[:, 1, 0], T[23]).then_inc(disc_taken, 1)
            ts(T[3], T[22], -1.0, ALU.add)
            for o, a, b, alu in ((28, 3, 23, ALU.add), (29, 23, 3, ALU.subtract)):
                tt(T[25], T[a], LR, ALU.mult)
                tt(T[26], T[b], LI, ALU.mult)
                tt(T[27], T[25], T[26], alu)
                tt(T[o], T[27], T[21], ALU.mult)

            def wide(ap):
                return ap.unsqueeze(2).to_broadcast([P, PAIRS, GROUP])

            pool.wait_ge(params_loaded, 16 * 6)
            do(pool.memset(bb[:], 0.0))
            for ri, (b0, b1, alu) in enumerate(((0, 1, ALU.subtract), (1, 0, ALU.add))):
                tt(prod[:, 0], b_nat[:, b0], wide(T[28]), ALU.mult)
                tt(prod[:, 1], b_nat[:, b1], wide(T[29]), ALU.mult)
                for g2 in range(2):
                    half = slice(64 * g2, 64 * g2 + 64)
                    ins = pool.tensor_tensor(bb[half, ri, :, g2, :], prod[half, 0], prod[half, 1], alu)
                    if (ri, g2) != (1, 1):
                        do(ins)
            ins.then_inc(b_bar_ready, 1)
            pool.wait_ge(b_bar_ready, 1)
            do(pool.memset(cb[:], 0.0))
            for g2 in range(2):
                half = slice(64 * g2, 64 * g2 + 64)
                chain.step(pool.tensor_copy(cb[half, 0, :, g2, :], c_nat[half, 0]))
                ins = pool.tensor_scalar(cb[half, 1, :, g2, :], c_nat[half, 1], -1.0, None, ALU.mult)
                if g2 == 0:
                    chain.step(ins)
            ins.then_inc(s5_mats_ready, 1)
            pool.wait_ge(s5_mats_ready, 1)
            pool.tensor_tensor(dg[:], ident[:].unsqueeze(1).to_broadcast([P, KT, P]),
                               d_sb[:].unsqueeze(2).to_broadcast([P, KT, P]), ALU.mult).then_inc(s5_mats_ready, 1)
            def clear_squares(n):
                pool.wait_ge(norm_summed, n)
                do(pool.memset(square_sum[:], 0.0))

            def squares(ph, nt, per):
                def body(s, par):
                    pool.wait_ge(x_updated, ph.fin0 + s + 1)
                    reach(pool, squares_summed, ph.fin0 + s)
                    add_squares(s * nt, nt)

                pairs_of_strips(pool, ph, body, chain, per)

            def up(ph):
                def body(s, par):
                    n = ph.up0 + s
                    if isinstance(s, int) and s == 0:
                        pool.wait_ge(rstd_done, ph.norm)
                    pool.wait_ge(strip_reduced, ph.strip0 + s + 3)
                    reach(pool, hidden_split, n)
                    pool.tensor_tensor(value[:], reduced[:, 2:4], rstd[:].unsqueeze(1).to_broadcast([P, 2, SEQ]),
                                       ALU.mult).then_inc(value_scaled, 1)
                    pool.wait_ge(value_scaled, n + 1)
                    pool.wait_ge(gelu_done, n + 1)
                    pool.tensor_tensor(value[:], value[:], conv_acc[:], ALU.mult).then_inc(hidden_ready, 1)
                    pool.wait_ge(hidden_high, n + 1)
                    tiles = bass.ds(s * 2, 2)
                    pool.tensor_tensor(hs[:, tiles, 1, :], value[:], hs[:, tiles, 0, :].bitcast(F32), ALU.subtract
                                       ).then_inc(hidden_split, 1)

                pairs_of_strips(pool, ph, body)

            clear_squares(1)
            squares(GLU, 2, 2 * 2)
            up(UP0)
            clear_squares(2)
            squares(DOWN0, 4, 2 * 5)
            pool.wait_ge(scaled, KEY.scale0 + 1)
            do(pool.memset(mask[:], 0.0))
            for cols, base in ((slice(0, P), 0), (slice(P, 3 * P), P)):
                do(pool.affine_select(out=mask[:, cols], in_=mask[:, cols], compare_op=ALU.is_ge, fill=MASKED,
                                      base=base, pattern=[[-1, cols.stop - cols.start]], channel_multiplier=1))
            do(pool.memset(e16[:], 0.0))
            pool.affine_select(out=e16[:], in_=e16[:], compare_op=ALU.not_equal, fill=1.0, base=0,
                               pattern=[[-1, HEADS]], channel_multiplier=1).then_inc(masks_ready, 1)

            pool.wait_ge(masks_ready, 1)
            pool.wait_ge(c_ready, 1)
            pool.wait_ge(scaled, QRY.scale0 + QRY.strips)

            def stage(h, b):
                if not isinstance(h, int) or h >= 2:
                    pool.wait_ge(v_turned, h - 1)
                head = bass.ds(h, 1)
                chain.step(pool.tensor_copy(q_st[:, b], qT[:, head].rearrange("p o t -> p (o t)")))
                chain.step(pool.tensor_copy(v_st[:, b], vT[:, head].rearrange("p o t -> p (o t)")))
                pool.tensor_tensor(ck_st[:, b], c16[:, 0], e16[:, head].to_broadcast([HEADS, SEQ]), ALU.mult
                                   ).then_inc(head_staged, 1)

            stage(0, 0)
            stage(1, 1)
            with pool.Fori(0, HEADS // 2 - 1) as i:
                chain.enter(i, 4)
                stage(i * 2 + 2, 0)
                stage(i * 2 + 3, 1)
            chain.leave(HEADS // 2 - 1, 4)
            pool.wait_ge(scores_done, HEADS)
            pool.wait_ge(o_split, HEADS + 2)
            do(pool.memset(gate[:, :, 0:2], 0.0))
            clear_squares(3)
            squares(WO, 4, 2 * 5)
            up(UP1)
            clear_squares(4)
            squares(DOWN1, 4, 2 * 5)


def kernel(**inputs):
    import numpy as np
    import concourse.bacc as bacc
    from concourse.bass_utils import run_bass_kernel_spmd as run

    a = {k: np.asarray(v) for k, v in inputs.items()}

    def plain(w):
        k, n = w.shape
        return np.ascontiguousarray(w.reshape(k // 512, 4, P, n // 512, 512).transpose(3, 0, 2, 1, 4)
                                    ).reshape(-1, P, 2048)

    def paired(w):
        k, n = w.shape
        return np.ascontiguousarray(w.reshape(k // 512, 4, P, 2, n // 512, 256).transpose(4, 0, 2, 1, 3, 5)
                                    ).reshape(-1, P, 2048)

    def columns(v):
        return v.reshape(-1, P).T

    w_up = a["ffn_w_up"]
    arrays = {
        "xT": a["x"][0].T.reshape(KT, P, SEQ).transpose(1, 0, 2),
        "gains": np.stack([columns(v) for v in (a["a_norm"][0], a["ffn_norm"][0], a["kv_norm"], a["b_norm"][0],
                                                a["ffn_norm"][1], a["final_norm"])], axis=1),
        "w_in": plain(a["a_w_in"][0]),
        "w_glu": paired(a["a_w_glu"][0]),
        "w_k": plain(a["w_k"]),
        "w_v": plain(a["w_v"]),
        "w_f": a["w_f"].reshape(KT, P, HEADS).transpose(1, 0, 2),
        "b_f": a["b_f"].reshape(HEADS, 1),
        "w_q": plain(a["b_w_q"][0]),
        "w_o": plain(a["b_w_o"][0]),
        "w_up": np.concatenate([paired(w) for w in w_up]),
        "w_down": np.concatenate([plain(w) for w in a["ffn_w_down"]]),
        "conv": np.stack([np.stack([columns(v) for v in (*a["ffn_conv_w"][l], a["ffn_conv_b"][l])], axis=1)
                          for l in range(2)], axis=1),
        "skip_d": columns(a["a_d"][0].reshape(-1)),
        "lam": np.stack([columns(a["a_lambda_re"][0].reshape(-1)), columns(a["a_lambda_im"][0].reshape(-1))], axis=1),
        "log_step": a["a_log_step"][0].reshape(PAIRS, 2).T,
        "b_in": np.stack([a[n][0].reshape(PAIRS, P, GROUP).transpose(1, 0, 2) for n in ("a_b_re", "a_b_im")], axis=1),
        "c_out": np.stack([a[n][0].reshape(PAIRS, 2, GROUP, STATE).transpose(1, 3, 0, 2).reshape(P, PAIRS, GROUP)
                           for n in ("a_c_re", "a_c_im")], axis=1),
    }
    arrays = {k: np.ascontiguousarray(v) for k, v in arrays.items()}
    nc = bacc.Bacc("TRN2", target_bir_lowering=False, num_devices=1)
    args = [nc.dram_tensor(n, v.shape, F32, kind="ExternalInput").ap() for n, v in arrays.items()]
    names = list(arrays)
    by = dict(zip(names, args))
    o = nc.dram_tensor("out", (P, KT, SEQ), F32, kind="ExternalOutput").ap()
    trunk(nc, **by, out=o)
    r = run(nc, [arrays], core_ids=[0])
    got = r.results[0]["out"]
    return np.ascontiguousarray(got.transpose(1, 0, 2).reshape(D_MODEL, SEQ).T)[None]
```

```python
from contextlib import ExitStack

import concourse.bass as bass
from concourse import mybir

ALU = mybir.AluOpType
ACT = mybir.ActivationFunctionType
AX_X = mybir.AxisListType.X
F32 = mybir.dt.float32
F32R = mybir.dt.float32r
I32 = mybir.dt.int32

P = 128
D_MODEL = 2048
SEQ = 256
D_FF = 5632
HEADS = 16
HEAD_DIM = 128
CONV_WIDTH = 3
NORM_EPS = 1e-6
STATE = 64
GROUP = 16
KT = D_MODEL // P
FT = D_FF // P
PAIRS = D_MODEL // GROUP // 2
UNIT_KT = 4
RING = 2
HALVES = 2
STRIP = 512
BLOCK = 2
CHUNK = 64
CHUNKS = SEQ // BLOCK // CHUNK
LAST_PARTS = (40,)
SCALE = float(HEAD_DIM) ** -0.5
MASKED = -3.0e38
GAIN_A, GAIN_FFN0, GAIN_KV, GAIN_B, GAIN_FFN1, GAIN_FINAL = range(6)


class Phase:

    units = strips = scale_strips = fin_strips = up_strips = 0

    def __init__(self, kind, strips, kc, w, w0=0, norm=0, gain=None, layer=None, mul=1.0):
        self.kind, self.strips, self.kc = kind, strips, kc
        self.w, self.w0 = w, w0
        self.norm = norm
        self.gain = gain
        self.layer = layer
        self.mul = mul
        self.src = self.dst = None
        self.unit0, self.strip0 = Phase.units, Phase.strips
        self.scale0, self.fin0, self.up0 = Phase.scale_strips, Phase.fin_strips, Phase.up_strips
        Phase.units += strips * kc
        Phase.strips += strips
        Phase.scale_strips += strips * (kind == "scale")
        Phase.fin_strips += strips * (kind in ("glu", "fin"))
        Phase.up_strips += strips * (kind == "up")


class Chain:

    def __init__(self, eng, sem):
        self.eng, self.sem, self.base, self.local = eng, sem, 0, 0

    def step(self, ins):
        ins.then_inc(self.sem, 1)
        self.local += 1

    def wait(self):
        self.eng.wait_ge(self.sem, self.base + self.local)

    def enter(self, i, per):
        self.saved, self.base, self.local = self.base + self.local, self.base + self.local + i * per, 0

    def leave(self, rounds, per):
        assert self.local == per, (self.local, per)
        self.base, self.local = self.saved + rounds * per, 0


def trunk(nc, xT, gains, w_in, w_glu, w_k, w_v, w_f, b_f, w_q, w_o, w_up, w_down, conv, skip_d,
          lam, log_step, b_in, c_out, out):
    Phase.units = Phase.strips = Phase.scale_strips = Phase.up_strips = 0
    Phase.fin_strips = 4
    n_ffn_units = D_FF * 2 // STRIP * 4
    WIN = Phase("scale", 4, 4, w=w_in, w0=0, norm=1)
    GLU = Phase("glu", 8, 4, w=w_glu, w0=0, norm=0, gain=GAIN_FFN0)
    UP0 = Phase("up", 22, 4, w=w_up, w0=0, norm=2, layer=0)
    DOWN0 = Phase("fin", 4, 11, w=w_down, w0=0, norm=0, gain=GAIN_KV)
    KEY = Phase("scale", 4, 4, w=w_k, w0=0, norm=3)
    VAL = Phase("scale", 4, 4, w=w_v, w0=0, norm=0)
    QRY = Phase("scale", 4, 4, w=w_q, w0=0, norm=0)
    WO = Phase("fin", 4, 4, w=w_o, w0=0, norm=0, gain=GAIN_FFN1)
    UP1 = Phase("up", 22, 4, w=w_up, w0=n_ffn_units, norm=4, layer=1)
    DOWN1 = Phase("fin", 4, 11, w=w_down, w0=44, norm=0, gain=GAIN_FINAL)
    PHASES = [WIN, GLU, UP0, DOWN0, KEY, VAL, QRY, WO, UP1, DOWN1]

    with ExitStack() as ctx:
        def sb(name, shape, dt=F32, stack=ctx):
            return stack.enter_context(nc.sbuf_tensor(name, shape, dt))

        def sem(name):
            return ctx.enter_context(nc.semaphore(name))

        acc = ctx.enter_context(nc.psum_tensor("acc", [P, 2, 4, 512], F32))

        x = sb("x", [P, KT, SEQ])
        with ExitStack() as s:
            u_blocks = sb("u_blocks", [P, KT, 2, SEQ // BLOCK], F32, s)
        raw = sb("raw", [P, 2, UNIT_KT, STRIP])
        with ExitStack() as s:
            cb = sb("cb", [P, BLOCK, 2, PAIRS, 2, GROUP], F32, s)
        w_high = sb("w_high", [P, 2, UNIT_KT, STRIP], F32R)
        w_low = sb("w_low", [P, 2, UNIT_KT, STRIP], F32R)
        reduced = sb("reduced", [P, 4, SEQ])
        xg = sb("xg", [P, 4, SEQ])
        square_sum = sb("square_sum", [P, SEQ])
        rstd = sb("rstd", [P, SEQ])
        ones = sb("ones", [P, P])
        ident = sb("ident", [P, P])
        eps = sb("eps", [P, 1])
        g_sb = sb("g_sb", [P, 6, KT])
        conv_sb = sb("conv_sb", [P, 2, CONV_WIDTH + 1, FT])
        d_sb = sb("d_sb", [P, KT])
        a4 = sb("a4", [P, 2, 2, PAIRS])
        wf_sb = sb("wf_sb", [P, KT, HEADS])
        bf_sb = sb("bf_sb", [HEADS, 1])
        with ExitStack() as s:
            b_nat = sb("b_nat", [P, 2, PAIRS, GROUP], F32, s)
        with ExitStack() as s:
            kd = sb("kd", [P, KT, P], F32, s)
        with ExitStack() as s:
            square = sb("square", [P, 2, SEQ], F32, s)
            gate = sb("gate", [P, 2, SEQ + 2], F32, s)
            conv_acc = sb("conv_acc", [P, 2, SEQ], F32, s)
            value = sb("value", [P, 2, SEQ], F32, s)
        with ExitStack() as s:
            q_st = sb("q_st", [P, 2, SEQ], F32, s)
            v_st = sb("v_st", [P, 2, SEQ], F32, s)
            ck_st = sb("ck_st", [HEADS, 2, SEQ], F32, s)
            v_tok = sb("v_tok", [P, 2, SEQ], F32, s)
        sb("epilogue_room", [P, 2 * 4 * SEQ + 8])
        with ExitStack() as s:
            st1 = sb("st1", [P, CHUNK, 2, PAIRS], F32, s)
        xs = sb("xs", [P, KT, 2, SEQ], F32R)
        with ExitStack() as s:
            u = sb("u", [P, KT, SEQ], F32, s)
            with ExitStack() as s2:
                bb = sb("bb", [P, KT, 2, 2, 2, BLOCK, 2 * GROUP], F32, s2)
            with ExitStack() as s2:
                bt = sb("bt", [P, KT, 2, 2, P], F32, s2)
            ys = sb("ys", [P, KT, 2, SEQ], F32R, s)
            with ExitStack() as s2:
                c_nat = sb("c_nat", [P, 2, PAIRS, GROUP], F32, s2)
            dg = sb("dg", [P, KT, P], F32, s)
            with ExitStack() as s2:
                with ExitStack() as s3:
                    squares_in = sb("squares_in", [P, KT, SEQ], F32, s3)
                c_pad = sb("c_pad", [P, 2, PAIRS, 2, GROUP], F32, s2)
                prod = sb("prod", [P, 2, PAIRS, GROUP], F32, s2)
                scr = sb("scr", [P, 30, PAIRS], F32, s2)
                scr_i = sb("scr_i", [P, PAIRS], I32, s2)
            st0 = sb("st0", [P, CHUNK, 2, PAIRS], F32, s)
        with ExitStack() as s:
            xq = sb("xq", [P, KT, 2, SEQ], F32R, s)
            kT = sb("kT", [P, HEADS, SEQ], F32, s)
            vT = sb("vT", [P, HEADS, SEQ], F32, s)
            qT = sb("qT", [P, HEADS, SEQ], F32, s)
            c16 = sb("c16", [HEADS, 5, SEQ], F32, s)
            mask = sb("mask", [P, 3 * P], F32, s)
        with ExitStack() as s:
            os_ = sb("os", [P, HEADS, 2, SEQ], F32R, s)
        hs = sb("hs", [P, FT, 2, SEQ], F32R)
        pr = reduced[:].rearrange("p b t -> p (b t)")[:, 0:6 * P].rearrange("p (b k) -> p b k", b=2)
        pt = xg[:].rearrange("p b t -> p (b t)")[:, 0:6 * P].rearrange("p (b k) -> p b k", b=2)
        e16 = sb("e16", [HEADS, HEADS])
        cq = sb("cq", [P, 2, HEADS])
        negmax = sb("negmax", [P, 2, 2])
        row_sum = sb("row_sum", [P, 2, 2])
        row_inv = sb("row_inv", [P, 2, 2])

        WIN.src, GLU.src, UP0.src, DOWN0.src = xs, ys, xs, hs
        KEY.src, VAL.src, QRY.src, WO.src, UP1.src, DOWN1.src = xs, xs, xq, os_, xs, hs
        WIN.dst, KEY.dst, VAL.dst, QRY.dst = u, kT, vT, qT
        QRY.mul = SCALE

        x_loaded = [sem(f"x_loaded{c}") for c in range(4)]
        gains_loaded = sem("gains_loaded")
        rates_loaded = sem("rates_loaded")
        params_loaded = sem("params_loaded")
        raw_loaded = [sem("raw_loaded0"), sem("raw_loaded1")]
        w_high_done = sem("w_high_done")
        w_split = sem("w_split")
        weights_used = sem("weights_used")
        strip_reduced = sem("strip_reduced")
        scaled = sem("scaled")
        sigmoid_done = sem("sigmoid_done")
        glu_done = sem("glu_done")
        x_updated = sem("x_updated")
        gained = sem("gained")
        x_high = sem("x_high")
        x_split = sem("x_split")
        squares_summed = sem("squares_summed")
        norm_summed = sem("norm_summed")
        root_done = sem("root_done")
        rstd_done = sem("rstd_done")
        gate_scaled = sem("gate_scaled")
        value_scaled = sem("value_scaled")
        conv_started = sem("conv_started")
        conv_done = sem("conv_done")
        gelu_done = sem("gelu_done")
        hidden_ready = sem("hidden_ready")
        hidden_high = sem("hidden_high")
        hidden_split = sem("hidden_split")
        consts_done = sem("consts_done")
        dve_chain = sem("dve_chain")
        pool_chain = sem("pool_chain")
        angle_ready = sem("angle_ready")
        trig_done = sem("trig_done")
        disc_ready = sem("disc_ready")
        disc_taken = sem("disc_taken")
        coef_ready = sem("coef_ready")
        b_bar_ready = sem("b_bar_ready")
        squared = sem("squared")
        c_cleared = sem("c_cleared")
        c_placed = sem("c_placed")
        s5_mats_ready = sem("s5_mats_ready")
        s5_filled = sem("s5_filled")
        s5_evacuated = sem("s5_evacuated")
        u_moved = sem("u_moved")
        scan_step = sem("scan_step")
        carried = sem("carried")
        y_high = sem("y_high")
        y_split = sem("y_split")
        xq_gained = sem("xq_gained")
        xq_high = sem("xq_high")
        xq_split = sem("xq_split")
        gate_logits = sem("gate_logits")
        gate_taken = sem("gate_taken")
        abs_ready = sem("abs_ready")
        soft_done = sem("soft_done")
        c_ready = sem("c_ready")
        masks_ready = sem("masks_ready")
        cq_turned = sem("cq_turned")
        cq_taken = sem("cq_taken")
        head_staged = sem("head_staged")
        scores_done = sem("scores_done")
        v_turned = sem("v_turned")
        v_taken = sem("v_taken")
        max_done = sem("max_done")
        exp_done = sem("exp_done")
        probs_ready = sem("probs_ready")
        probs_turned = sem("probs_turned")
        probs_taken = sem("probs_taken")
        o_done = sem("o_done")
        o_high = sem("o_high")
        o_split = sem("o_split")
        out_ready = sem("out_ready")
        stored = sem("stored")

        def reach(eng, s, count):
            if isinstance(count, int) and count <= 0:
                return
            eng.wait_ge(s, count)

        def pairs_of_strips(eng, ph, body, chain=None, per=0, peel=1):
            for s in range(2 * peel):
                body(s, s % 2)
            rest = ph.strips // 2 - peel
            if rest == 1:
                body(2 * peel, 0)
                body(2 * peel + 1, 1)
            elif rest > 1:
                with eng.Fori(0, rest) as i:
                    if chain:
                        chain.enter(i, per)
                    body(i * 2 + 2 * peel, 0)
                    body(i * 2 + 2 * peel + 1, 1)
                if chain:
                    chain.leave(rest, per)

        def units_through(ph, s):
            return HALVES * RING + (ph.unit0 + ph.kc) * HALVES + s * (ph.kc * HALVES)

        def half_unit(ph, s, c, h):
            return (ph.unit0 + c) * HALVES + h + s * (ph.kc * HALVES)

        def half_tiles(h):
            return slice(h * UNIT_KT // HALVES, (h + 1) * UNIT_KT // HALVES)

        def reduced_free(eng, ph, s):
            if isinstance(s, int) and s == 0:
                at = PHASES.index(ph)
                if at == 0:
                    return
                ph, s = PHASES[at - 1], PHASES[at - 1].strips
            if ph.kind == "scale":
                reach(eng, scaled, ph.scale0 + s)
            elif ph.kind == "up":
                reach(eng, gate_scaled, ph.up0 + s)
                reach(eng, value_scaled, ph.up0 + s)
            else:
                reach(eng, x_updated, ph.fin0 + s)

        block = ctx.enter_context(nc.Block())

        @block.sync
        def _(sp):
            def load(ph, i, slot):
                sp.wait_ge(w_split, i * (2 * HALVES) + (ph.unit0 + slot + 1) * HALVES)
                sp.dma_start(raw[:, slot].rearrange("p k n -> p (k n)"),
                             ph.w[bass.ds(i * 2 + (ph.w0 + slot), 1)].rearrange("o p n -> (o p) n")
                             ).then_inc(raw_loaded[slot], 16)

            def load_x(c):
                sp.dma_start(x[:, 4 * c:4 * c + 4], xT[:, 4 * c:4 * c + 4]).then_inc(x_loaded[c], 16)

            load_x(0)
            load(WIN, 0, 0)
            load_x(1)
            for ri in range(2):
                sp.dma_start(scr[:, ri], lam[:, ri]).then_inc(rates_loaded, 16)
            for g2 in range(2):
                sp.dma_start(scr[64 * g2:64 * g2 + 64, 2],
                             log_step[g2:g2 + 1, :].to_broadcast([64, PAIRS])).then_inc(rates_loaded, 16)
            load(WIN, 0, 1)
            load_x(2)
            load_x(3)
            for dst, src in ((b_nat, b_in), (c_nat, c_out), (conv_sb, conv), (d_sb, skip_d), (wf_sb, w_f),
                             (bf_sb, b_f)):
                sp.dma_start(dst[:], src).then_inc(params_loaded, 16)
            for ph in PHASES:
                if ph is GLU:
                    sp.wait_ge(s5_filled, 5 + 4 * CHUNKS)
                before = 1 if ph is WIN else 0
                with sp.Fori(0, ph.strips * ph.kc // 2 - before) as i:
                    for slot in range(2):
                        load(ph, i + before, slot)
            for c in range(4):
                sp.wait_ge(out_ready, c + 1)
                sp.dma_start(out[:, 4 * c:4 * c + 4], x[:, 4 * c:4 * c + 4]).then_inc(stored, 16)
            sp.wait_ge(stored, 64)

        @block.tensor
        def _(pe):
            pe.sem_inc(weights_used, RING * HALVES)
            pe.wait_ge(consts_done, 2)

            def unit(ph, s, par, c, last_bank_wait=None):
                slot = (par * ph.kc + c) % 2
                for k in range(UNIT_KT):
                    if k % (UNIT_KT // HALVES) == 0:
                        pe.wait_ge(w_split, half_unit(ph, s, c, k * HALVES // UNIT_KT) + RING * HALVES + 1)
                    for m in range(4):
                        if last_bank_wait and c == 0 and k == 0 and m == 3:
                            pe.wait_ge(*last_bank_wait)
                        kt = c * UNIT_KT + k
                        cols = slice(m * P, (m + 1) * P)
                        first, last = kt == 0, kt == ph.kc * UNIT_KT - 1
                        pe.matmul(acc[:, par, m, :], w_high[:, slot, k, cols],
                                  ph.src[:, kt].rearrange("p h t -> p (h t)"),
                                  start=first, stop=last, skip_group_check=True)
                        mm = pe.matmul(acc[:, par, m, 0:SEQ], w_low[:, slot, k, cols],
                                       ph.src[:, kt, 0], start=False, stop=last,
                                       skip_group_check=True)
                    if (k + 1) % (UNIT_KT // HALVES) == 0:
                        mm.then_inc(weights_used, 1)

            def input_ready(ph, c):
                if ph is WIN:
                    pe.wait_ge(x_split, c + 1)
                elif ph is GLU:
                    pe.wait_ge(y_split, c + 1)
                elif ph is UP0 or ph is UP1:
                    before = GLU if ph is UP0 else WO
                    per = before.strips // 4
                    pe.wait_ge(x_split, before.fin0 + per * (c + 1))
                elif ph is DOWN0 or ph is DOWN1:
                    before = UP0 if ph is DOWN0 else UP1
                    pe.wait_ge(hidden_split, before.up0 + 2 * (c + 1))
                elif ph is KEY:
                    pe.wait_ge(x_split, DOWN0.fin0 + c + 1)
                elif ph is QRY:
                    pe.wait_ge(xq_split, c + 1)
                elif ph is WO:
                    pe.wait_ge(o_split, 4 * c + 4 + 2)

            def phase(ph):
                def strip(s, par, first=False, wait3=None):
                    pe.wait_ge(strip_reduced, ph.strip0 + s + 1)
                    for c in range(ph.kc):
                        if first:
                            input_ready(ph, c)
                        unit(ph, s, par, c, wait3)

                strip(0, 0, True)
                if ph.norm:
                    pe.wait_ge(strip_reduced, ph.strip0 + 2)
                    fin_before = {1: 4, 2: GLU.fin0 + 8, 3: DOWN0.fin0 + 4, 4: WO.fin0 + 4}[ph.norm]
                    pe.wait_ge(squares_summed, fin_before)
                    pe.matmul(acc[:, 1, 3, 0:SEQ], ones[:], square_sum[:], start=True, stop=True
                              ).then_inc(norm_summed, 1)
                    strip(1, 1, False, (root_done, ph.norm))
                else:
                    strip(1, 1)
                rest = ph.strips // 2 - 1
                if rest == 1:
                    strip(2, 0)
                    strip(3, 1)
                else:
                    with pe.Fori(0, rest) as i:
                        strip(i * 2 + 2, 0)
                        strip(i * 2 + 3, 1)

            def s5():
                fills = [0]

                def begin():
                    k = fills[0]
                    if k < 2:
                        pe.wait_ge(strip_reduced, WIN.strips + 1 + k)
                    else:
                        pe.wait_ge(s5_evacuated, k - 1)
                    fills[0] += 1
                    return k % 2

                pe.wait_ge(b_bar_ready, 1)
                pe.wait_ge(c_placed, 1)
                par = begin()
                for q in range(PAIRS):
                    rows = slice(32 * (q % 4), 32 * (q % 4) + 32)
                    for ri in range(2):
                        ins = pe.matmul(acc[rows, par, 0, (q // 4) * 32:(q // 4 + 1) * 32],
                                        bb[:, q // 4, q % 4 // 2, ri, q % 2, BLOCK - 1],
                                        c_pad[:, ri, q].rearrange("p g c -> p (g c)"),
                                        start=(ri == 0), stop=(ri == 1), skip_group_check=True)
                ins.then_inc(s5_filled, 1)
                for f in range(4):
                    par = begin()
                    for m in range(4):
                        for e in range(2):
                            for ri in range(2):
                                col = (2 * e + ri) * P
                                ins = pe.transpose(acc[:, par, m, col:col + P],
                                                   bb[:, 4 * f + m, e, ri].rearrange("p b l c -> p (b l c)"),
                                                   ident[:])
                    ins.then_inc(s5_filled, 1)

                def tokens(c, tau):
                    return slice(c * CHUNK * BLOCK + tau, (c + 1) * CHUNK * BLOCK, BLOCK)

                def inputs(c):
                    for grp in range(4):
                        par = begin()
                        for m in range(4):
                            mt = grp * 4 + m
                            for ri in range(2):
                                col = (m * 2 + ri) * CHUNK
                                for e in range(2):
                                    for b in range(2):
                                        rows = slice(64 * b, 64 * b + 64)
                                        ins = pe.matmul(acc[:, par, 2 * e + b, col:col + CHUNK],
                                                        bt[rows, mt, e, ri],
                                                        u_blocks[rows, mt, e, c * CHUNK:(c + 1) * CHUNK],
                                                        start=True, stop=True)
                        ins.then_inc(s5_filled, 1)

                def outputs(c):
                    st = (st0, st1)[c]
                    sets = [begin(), begin()]

                    def place(mt, tau):
                        c0 = mt % (KT // 2) * CHUNK
                        return acc[:, sets[mt // (KT // 2)], tau, c0:c0 + CHUNK]

                    def c_rows(power, ri, q):
                        return cb[:, power, ri, q].rearrange("p g c -> p (g c)")

                    for mt in range(KT):
                        for tau in range(BLOCK):
                            pe.matmul(place(mt, tau), dg[:, mt, :], u[:, mt, tokens(c, tau)],
                                      start=(mt % (KT // 2) == 0), stop=False, skip_group_check=True)
                        pe.matmul(place(mt, 0), kd[:, mt, :], u[:, mt, tokens(c, 0)],
                                  start=False, stop=False, skip_group_check=True)
                        if c > 0:
                            for j in range(4):
                                for ri in range(2):
                                    pe.matmul(place(mt, 0)[32 * j:32 * j + 32, 0:1], c_rows(1, ri, 4 * mt + j),
                                              st0[:, CHUNK - 1:CHUNK, ri, 4 * mt + j],
                                              start=False, stop=False, skip_group_check=True)
                    bounds = (0, CHUNK) if c < CHUNKS - 1 else (0, *LAST_PARTS, CHUNK)
                    for b0, b1 in zip(bounds, bounds[1:]):
                        pe.wait_ge(scan_step, 1 + 3 * (c * CHUNK + b1 - 1))
                        lead = max(b0, 1)
                        for mt in range(KT):
                            for j in range(4):
                                q = 4 * mt + j
                                rows = slice(32 * j, 32 * j + 32)
                                for ri in range(2):
                                    pe.matmul(place(mt, 0)[rows, lead:b1], c_rows(1, ri, q),
                                              st[:, lead - 1:b1 - 1, ri, q],
                                              start=False, stop=(ri == 1), skip_group_check=True)
                                    ins = pe.matmul(place(mt, 1)[rows, b0:b1], c_rows(0, ri, q), st[:, b0:b1, ri, q],
                                                    start=False, stop=(ri == 1), skip_group_check=True)
                            if b1 == CHUNK and mt % (KT // 2) == KT // 2 - 1:
                                ins.then_inc(s5_filled, 1)

                pe.wait_ge(s5_evacuated, 5)
                pe.wait_ge(u_moved, 8)
                inputs(0)
                inputs(1)
                pe.wait_ge(s5_mats_ready, 1)
                pe.wait_ge(c_placed, 2)
                for c in range(CHUNKS):
                    outputs(c)
                pe.wait_ge(s5_evacuated, fills[0])

            def forget_gate():
                pe.wait_ge(params_loaded, 16 * 6)
                pe.wait_ge(strip_reduced, VAL.strip0 + VAL.strips + 1)
                for kt in range(KT):
                    ins = pe.matmul(acc[0:HEADS, 0, 0, :], wf_sb[:, kt, :],
                                    xs[:, kt].rearrange("p h t -> p (h t)").bitcast(F32),
                                    start=(kt == 0), stop=(kt == KT - 1))
                ins.then_inc(gate_logits, 1)
                pe.wait_ge(gate_taken, 1)

            def attention():
                pe.wait_ge(strip_reduced, QRY.strip0 + QRY.strips + 2)
                pe.wait_ge(c_ready, 1)
                for qb in range(2):
                    ins = pe.transpose(acc[:, 0, 0, qb * HEADS:(qb + 1) * HEADS],
                                       c16[:, 1, qb * P:(qb + 1) * P], ident[0:HEADS, 0:HEADS])
                ins.then_inc(cq_turned, 1)
                pe.wait_ge(cq_taken, 1)

                def scores(h, b):
                    pe.wait_ge(head_staged, h + 1)
                    if not isinstance(h, int) or h >= 2:
                        pe.wait_ge(max_done, h - 1)
                        pe.wait_ge(v_taken, h - 1)
                    s_bank = acc[:, b, 0]
                    pe.matmul(s_bank[:, 0:P], q_st[:, b, 0:P], kT[:, bass.ds(h, 1), 0:P].rearrange("p o t -> p (o t)"),
                              start=True, stop=False)
                    pe.matmul(s_bank[:, 0:P], ones[0:HEADS, :], ck_st[:, b, 0:P], start=False, stop=True)
                    pe.matmul(s_bank[:, P:3 * P], q_st[:, b, P:2 * P],
                              kT[:, bass.ds(h, 1), :].rearrange("p o t -> p (o t)"), start=True, stop=False)
                    pe.matmul(s_bank[:, P:3 * P], ones[0:HEADS, :], ck_st[:, b, :], start=False, stop=True
                              ).then_inc(scores_done, 1)
                    pe.transpose(acc[:, b, 1, 0:P], v_st[:, b, 0:P], ident[:])
                    pe.transpose(acc[:, b, 1, P:2 * P], v_st[:, b, P:2 * P], ident[:]).then_inc(v_turned, 1)

                def turn(h, b):
                    pe.wait_ge(probs_ready, h + 1)
                    pe.wait_ge(probs_taken, h + 1)
                    for j in range(3):
                        ins = pe.transpose(acc[:, b, 2, j * P:(j + 1) * P], pr[:, b, j * P:(j + 1) * P], ident[:])
                    ins.then_inc(probs_turned, 1)

                def mix(h, b):
                    pe.wait_ge(probs_taken, h + 3)
                    pe.wait_ge(v_taken, h + 1)
                    pe.wait_ge(o_split, h + 1)
                    pe.matmul(acc[:, b, 3, 0:SEQ], v_tok[:, b, 0:P], pt[:, b, 0:SEQ], start=True, stop=False,
                              skip_group_check=True)
                    pe.matmul(acc[:, b, 3, P:SEQ], v_tok[:, b, P:SEQ], pt[:, b, SEQ:3 * P], start=False,
                              stop=True, skip_group_check=True).then_inc(o_done, 1)

                scores(0, 0)
                scores(1, 1)
                turn(0, 0)
                with pe.Fori(0, HEADS // 2 - 1) as i:
                    for b in range(2):
                        scores(i * 2 + (b + 2), b)
                        turn(i * 2 + (b + 1), 1 - b)
                        mix(i * 2 + b, b)
                turn(HEADS - 1, 1)
                mix(HEADS - 2, 0)
                mix(HEADS - 1, 1)
                pe.wait_ge(o_split, HEADS + 2)

            phase(WIN)
            s5()
            phase(GLU)
            phase(UP0)
            phase(DOWN0)
            phase(KEY)
            phase(VAL)
            forget_gate()
            phase(QRY)
            attention()
            phase(WO)
            phase(UP1)
            phase(DOWN1)
            pe.wait_ge(squares_summed, DOWN1.fin0 + DOWN1.strips)
            pe.wait_ge(strip_reduced, DOWN1.strip0 + DOWN1.strips + 2)
            pe.matmul(acc[:, 1, 3, 0:SEQ], ones[:], square_sum[:], start=True, stop=True).then_inc(norm_summed, 1)

        @block.scalar
        def _(act):
            act.dma_start(g_sb[:], gains).then_inc(gains_loaded, 16)

            def high(ph, s, par, c):
                slot = (par * ph.kc + c) % 2
                act.wait_ge(raw_loaded[slot], loads(ph, s, par, c))
                for h in range(HALVES):
                    act.wait_ge(weights_used, half_unit(ph, s, c, h) + 1)
                    act.activation(w_high[:, slot, half_tiles(h)], raw[:, slot, half_tiles(h)], ACT.Copy
                                   ).then_inc(w_high_done, 1)

            def loads(ph, s, par, c):
                return (s - par) * (8 * ph.kc) + 16 * ((ph.unit0 + par * ph.kc + c) // 2 + 1)

            def rms_root(n):
                act.wait_ge(norm_summed, n)
                act.activation(rstd[:], acc[:, 1, 3, 0:SEQ], ACT.Sqrt, bias=eps[:], scale=1.0 / D_MODEL
                               ).then_inc(root_done, 1)

            def fin_high(n, tile, nt):
                act.wait_ge(gained, n + 1)
                act.activation(xs[:, bass.ds(tile, nt), 0, :], xg[:, 0:nt], ACT.Copy).then_inc(x_high, 1)

            def epilogue(ph, s, slot):
                if ph.kind == "glu":
                    if slot == 0:
                        act.wait_ge(strip_reduced, ph.strip0 + s + 3)
                        act.activation(value[:], reduced[:, 2:4], ACT.Sigmoid).then_inc(sigmoid_done, 1)
                    if slot == 2:
                        fin_high(ph.fin0 + s, s * 2, 2)
                elif ph.kind == "fin":
                    if slot == 1 and ph is not DOWN1:
                        fin_high(ph.fin0 + s, s * 4, 4)
                elif ph.kind == "up":
                    n = ph.up0 + s
                    if slot == 0:
                        act.wait_ge(gate_scaled, n + 1)
                        reach(act, hidden_ready, n)
                        for j in range(2):
                            ins = act.activation(conv_acc[:, j], gate[:, j, 2:SEQ + 2], ACT.Identity,
                                                 bias=conv_sb[:, ph.layer, 3, bass.ds(s * 2 + j, 1)],
                                                 scale=conv_sb[:, ph.layer, 2, bass.ds(s * 2 + j, 1)])
                        ins.then_inc(conv_started, 1)
                    if slot == 2:
                        act.wait_ge(conv_done, n + 1)
                        act.activation(conv_acc[:], conv_acc[:], ACT.Gelu_apprx_tanh).then_inc(gelu_done, 1)
                        act.wait_ge(hidden_ready, n + 1)
                        act.activation(hs[:, bass.ds(s * 2, 2), 0, :], value[:], ACT.Copy
                                       ).then_inc(hidden_high, 1)

            def phase(ph, before):
                def strip(s, par, prev):
                    for c in range(ph.kc):
                        if ph.norm and isinstance(s, int) and s == 1 and c == 1:
                            rms_root(ph.norm)
                        high(ph, s, par, c)
                        if c == 0 and prev is bring_in:
                            prev(-1)
                        if 1 <= c <= 3:
                            prev(c - 1)
                            if ph is WIN:
                                discretise(s, c - 1)

                def body(s, par):
                    first = isinstance(s, int) and s == 0
                    strip(s, par, before if first else (lambda slot: epilogue(ph, s - 1, slot)))

                pairs_of_strips(act, ph, body)
                return lambda slot: epilogue(ph, ph.strips - 1, slot)

            def s5():
                act.wait_ge(c_placed, 1)
                act.wait_ge(weights_used, HALVES * (RING + WIN.strips * WIN.kc))
                act.activation(cb[:, 0], c_pad[:], ACT.Copy).then_inc(c_placed, 1)
                act.wait_ge(s5_filled, 1)
                for j in range(4):
                    rows = slice(32 * j, 32 * j + 32)
                    ins = act.activation(kd[rows, :, rows], acc[rows, 0, 0].rearrange("p (m c) -> p m c", m=KT),
                                         ACT.Copy)
                ins.then_inc(s5_evacuated, 1)
                for f in range(4):
                    act.wait_ge(s5_filled, f + 2)
                    act.activation(bt[:, 4 * f:4 * f + 4].rearrange("p m e r s -> p m (e r s)"),
                                   acc[:, (f + 1) % 2], ACT.Copy).then_inc(s5_evacuated, 1)
                fills = [5]

                def inputs(c):
                    st = (st0, st1)[c]
                    for grp in range(4):
                        par = fills[0] % 2
                        fills[0] += 1
                        act.wait_ge(s5_filled, fills[0])
                        for j in range(4):
                            q0 = grp * 16 + j
                            dst = st[:, :, :, q0:q0 + 13:4].rearrange("p t r m -> p m r t")
                            ins = act.activation(dst, acc[:, par, j].rearrange(
                                "p (m r t) -> p m r t", m=4, r=2), ACT.Copy)
                        ins.then_inc(s5_evacuated, 1)

                def outputs(c, half):
                    par = fills[0] % 2
                    fills[0] += 1
                    act.wait_ge(s5_filled, fills[0])
                    for tau in range(BLOCK):
                        ins = act.activation(u[:, 8 * half:8 * half + 8,
                                               c * CHUNK * BLOCK + tau:(c + 1) * CHUNK * BLOCK:BLOCK],
                                             acc[:, par, tau].rearrange("p (m t) -> p m t", m=8),
                                             ACT.Gelu_apprx_tanh)
                    ins.then_inc(s5_evacuated, 1)

                inputs(0)
                inputs(1)
                for c in range(CHUNKS):
                    for half in range(2):
                        outputs(c, half)
                        if c == CHUNKS - 1:
                            act.wait_ge(s5_evacuated, fills[0])
                            for part in (2 * half, 2 * half + 1):
                                act.activation(ys[:, 4 * part:4 * part + 4, 0, :], u[:, 4 * part:4 * part + 4],
                                               ACT.Copy).then_inc(y_high, 1)

            def log_sigmoid():
                act.wait_ge(abs_ready, 1)
                act.activation(c16[:, 2], c16[:, 3], ACT.Exp, scale=-1.0).then_inc(soft_done, 1)
                act.wait_ge(abs_ready, 2)
                act.activation(c16[:, 3], c16[:, 4], ACT.Ln).then_inc(soft_done, 1)

            def attention():
                act.wait_ge(cq_turned, 1)
                act.activation(cq[:], acc[:, 0, 0, 0:2 * HEADS].rearrange("p (b h) -> p b h", b=2), ACT.Copy
                               ).then_inc(cq_taken, 1)

                def exps(h, b):
                    act.wait_ge(max_done, h + 1)
                    for j, cols in ((0, slice(0, P)), (1, slice(P, 3 * P))):
                        ins = act.activation(pr[:, b, cols], pr[:, b, cols], ACT.Exp, bias=negmax[:, b, j:j + 1],
                                             accum_out=row_sum[:, b, j:j + 1])
                    ins.then_inc(exp_done, 1)

                def take_v(h, b):
                    act.wait_ge(v_turned, h + 1)
                    act.wait_ge(o_done, h + 1)
                    act.activation(v_tok[:, b], acc[:, b, 1, 0:SEQ], ACT.Copy).then_inc(v_taken, 1)

                def take_probs(h, b):
                    act.wait_ge(probs_turned, h + 1)
                    act.wait_ge(o_done, h + 1)
                    act.activation(pt[:, b], acc[:, b, 2, 0:3 * P], ACT.Copy).then_inc(probs_taken, 1)

                def take_o(h, b):
                    act.wait_ge(o_done, h + 3)
                    act.activation(os_[:, bass.ds(h, 1), 0, :].rearrange("p o t -> p (o t)"),
                                   acc[:, b, 3, 0:SEQ], ACT.Copy).then_inc(o_high, 1)

                exps(0, 0)
                take_v(0, 0)
                exps(1, 1)
                take_probs(0, 0)
                take_v(1, 1)
                with act.Fori(0, HEADS // 2 - 1) as i:
                    for b in range(2):
                        exps(i * 2 + (b + 2), b)
                        take_probs(i * 2 + (b + 1), 1 - b)
                        take_o(i * 2 + b, b)
                        take_v(i * 2 + (b + 2), b)
                take_probs(HEADS - 1, 1)
                take_o(HEADS - 2, 0)
                take_o(HEADS - 1, 1)

            act.wait_ge(consts_done, 2)

            def bring(c):
                fin_high(c, 4 * c, 4)
                act.activation(squares_in[:, 4 * c:4 * c + 4], x[:, 4 * c:4 * c + 4], ACT.Square
                               ).then_inc(squared, 1)

            def bring_in(slot):
                if slot < 2:
                    bring(2 + slot)

            def discretise(s, slot):
                if (s, slot) == (1, 0):
                    act.wait_ge(angle_ready, 1)
                    act.activation(scr[:, 8], scr[:, 7], ACT.Sin)
                    act.activation(scr[:, 10], scr[:, 9], ACT.Sin).then_inc(trig_done, 1)
                elif (s, slot) == (2, 0):
                    act.wait_ge(params_loaded, 16 * 6)
                    act.wait_ge(c_cleared, 1)
                    for g2 in range(2):
                        half = slice(64 * g2, 64 * g2 + 64)
                        for ri in range(2):
                            ins = act.activation(c_pad[half, ri, :, g2, :], c_nat[half, ri], ACT.Copy,
                                                 scale=1.0 - 2.0 * ri)
                    ins.then_inc(c_placed, 1)

            bring(0)
            prev = phase(WIN, bring_in)

            for slot in range(3):
                prev(slot)
            s5()
            prev = phase(GLU, lambda slot: None)
            prev = phase(UP0, prev)
            prev = phase(DOWN0, prev)
            prev = phase(KEY, prev)

            def after_key(slot, prev=prev):
                prev(slot)
                act.wait_ge(xq_gained, slot + 1)
                act.activation(xq[:, 4 * slot:4 * slot + 4, 0, :], xg[:], ACT.Copy).then_inc(xq_high, 1)
                if slot == 2:
                    act.wait_ge(xq_gained, 4)
                    act.activation(xq[:, 12:16, 0, :], xg[:], ACT.Copy).then_inc(xq_high, 1)

            prev = phase(VAL, after_key)

            def after_value(slot, prev=prev):
                prev(slot)
                if slot == 0:
                    log_sigmoid()

            prev = phase(QRY, after_value)

            def after_query(slot, prev=prev):
                prev(slot)
                if slot == 0:
                    attention()

            prev = phase(WO, after_query)
            prev = phase(UP1, prev)
            prev = phase(DOWN1, prev)
            rms_root(5)

        @block.vector
        def _(dve):
            dve.sem_inc(w_split, RING * HALVES)
            dve.sem_inc(strip_reduced, 2)
            dve.sem_inc(scan_step, 1)
            dve.sem_inc(o_split, 2)
            dve.sem_inc(probs_taken, 2)
            dve.sem_inc(o_done, 2)
            dve.sem_inc(x_updated, 4)
            chain = Chain(dve, dve_chain)

            def low(ph, s, par, c):
                slot = (par * ph.kc + c) % 2
                for h in range(HALVES):
                    dve.wait_ge(w_high_done, half_unit(ph, s, c, h) + 1)
                    tiles = half_tiles(h)
                    dve.tensor_tensor(w_low[:, slot, tiles], raw[:, slot, tiles],
                                      w_high[:, slot, tiles].bitcast(F32), ALU.subtract).then_inc(w_split, 1)

            def rms_inverse(n):
                dve.wait_ge(root_done, n)
                dve.reciprocal(rstd[:], rstd[:]).then_inc(rstd_done, 1)
                dve.wait_ge(rstd_done, n)

            def all_rows(ap, k):
                return ap.unsqueeze(1).to_broadcast([P, k, SEQ])

            def reduce_strip(ph, s, par):
                dve.wait_ge(weights_used, units_through(ph, s))
                reduced_free(dve, ph, s)
                dve.tensor_reduce(reduced[:], acc[:, par].rearrange("p b (h t) -> p b t h", h=2), AX_X, ALU.add
                                  ).then_inc(strip_reduced, 1)
                dve.wait_ge(strip_reduced, ph.strip0 + s + 3)

            def gain(n, tile, nt, which):
                if n is not None:
                    dve.wait_ge(x_updated, n + 1)
                for j in range(nt):
                    ins = dve.tensor_scalar(xg[:, j], x[:, bass.ds(tile + j, 1)].rearrange("p o t -> p (o t)"),
                                            g_sb[:, which, bass.ds(tile + j, 1)], None, ALU.mult)
                return ins

            def fin_low(n, tile, nt):
                dve.wait_ge(x_high, n + 1)
                dve.tensor_tensor(xs[:, bass.ds(tile, nt), 1, :], xg[:, 0:nt],
                                  xs[:, bass.ds(tile, nt), 0, :].bitcast(F32), ALU.subtract).then_inc(x_split, 1)

            def epilogue(ph, s, par, slot):
                if ph.kind == "scale" and slot == 0:
                    reduce_strip(ph, s, par)
                    dst = ph.dst[:, bass.ds(s * 4, 4)]
                    if ph.mul == 1.0:
                        ins = dve.tensor_tensor(dst, reduced[:], all_rows(rstd[:], 4), ALU.mult)
                    else:
                        ins = dve.scalar_tensor_tensor(dst, reduced[:], ph.mul, all_rows(rstd[:], 4),
                                                       ALU.mult, ALU.mult)
                    ins.then_inc(scaled, 1)
                elif ph.kind == "glu":
                    n = ph.fin0 + s
                    if slot == 0:
                        reduce_strip(ph, s, par)
                    if slot == 1:
                        dve.wait_ge(sigmoid_done, s + 1)
                        dve.tensor_tensor(reduced[:, 0:2], reduced[:, 0:2], value[:], ALU.mult).then_inc(glu_done, 1)
                        dve.wait_ge(glu_done, s + 1)
                        tiles = x[:, bass.ds(s * 2, 2)]
                        dve.tensor_tensor(tiles, tiles, reduced[:, 0:2], ALU.add).then_inc(x_updated, 1)
                        dve.wait_ge(x_split, n)
                        gain(n, s * 2, 2, ph.gain).then_inc(gained, 1)
                    if slot == 2:
                        fin_low(n, s * 2, 2)
                elif ph.kind == "fin":
                    n = ph.fin0 + s
                    if slot == 0:
                        reduce_strip(ph, s, par)
                        tiles = x[:, bass.ds(s * 4, 4)]
                        dve.tensor_tensor(tiles, tiles, reduced[:], ALU.add).then_inc(x_updated, 1)
                        if ph is not DOWN1:
                            dve.wait_ge(x_split, n)
                            gain(n, s * 4, 4, ph.gain).then_inc(gained, 1)
                    if slot == 2 and ph is not DOWN1:
                        fin_low(n, s * 4, 4)
                elif ph.kind == "up":
                    n = ph.up0 + s
                    if slot == 0:
                        reduce_strip(ph, s, par)
                        reach(dve, conv_done, n)
                        dve.tensor_tensor(gate[:, :, 2:SEQ + 2], reduced[:, 0:2], all_rows(rstd[:], 2), ALU.mult
                                          ).then_inc(gate_scaled, 1)
                    if slot == 1:
                        dve.wait_ge(conv_started, n + 1)
                        for tap, order in ((1, 0), (0, 1)):
                            for j in range(2):
                                ins = dve.scalar_tensor_tensor(
                                    conv_acc[:, j], gate[:, j, tap:tap + SEQ],
                                    conv_sb[:, ph.layer, tap, bass.ds(s * 2 + j, 1)], conv_acc[:, j],
                                    ALU.mult, ALU.add)
                                if tap == 1:
                                    chain.step(ins)
                            if tap == 1:
                                chain.wait()
                        ins.then_inc(conv_done, 1)

            def phase(ph, before):
                def strip(s, par, prev):
                    for c in range(ph.kc):
                        low(ph, s, par, c)
                        if c == 0 and prev is bring_in:
                            prev(-1)
                        if 1 <= c <= 3:
                            if c == 1 and ph.norm and isinstance(s, int) and s == 1:
                                rms_inverse(ph.norm)
                            prev(c - 1)
                            if ph is WIN:
                                discretise(s, c - 1)

                def body(s, par):
                    first = isinstance(s, int) and s == 0
                    strip(s, par, before if first else (lambda slot: epilogue(ph, s - 1, 1 - par, slot)))

                pairs_of_strips(dve, ph, body, chain, 4 if ph.kind == "up" else 0)
                return lambda slot: epilogue(ph, ph.strips - 1, 1, slot)

            def s5():
                dve.wait_ge(scaled, WIN.strips)
                for j in range(4):
                    e, b = j // 2, j % 2
                    for tau in range(BLOCK):
                        row = 64 * b + 32 * tau
                        dve.tensor_copy(u_blocks[row:row + 32, :, e], u[32 * j:32 * j + 32, :, tau::BLOCK]
                                        ).then_inc(u_moved, 1)

                count = [0, 0]
                products = reduced[:, 0].rearrange("p (o i q) -> p o i q", o=2, i=2)
                sums = xg[:, 0, 0:2 * PAIRS].rearrange("p (o q) -> p o q", o=2)
                carry = xg[:, 1, 0:2 * PAIRS].rearrange("p (o q) -> p o q", o=2)

                def op(out_ap, a, b, alu):
                    dve.wait_ge(scan_step, count[0] + count[1] + 1)
                    dve.tensor_tensor(out_ap, a, b, alu).then_inc(scan_step, 1)
                    count[1] += 1

                def step(prev, cur):
                    op(products, a4[:], prev.unsqueeze(1).to_broadcast([P, 2, 2, PAIRS]), ALU.mult)
                    op(sums, cur, products[:, :, 0], ALU.add)
                    op(cur, sums, products[:, :, 1], ALU.add)

                for c in range(CHUNKS):
                    st = (st0, st1)[c]
                    dve.wait_ge(s5_evacuated, 5 + 4 * (c + 1))
                    if c == 0:
                        dve.wait_ge(disc_taken, 1)
                    else:
                        dve.wait_ge(carried, c)
                        step(carry, st[:, 0])
                    start, unroll = count[0] + count[1], 7
                    with dve.Fori(0, (CHUNK - 1) // unroll) as i:
                        count[0], count[1] = start + i * (3 * unroll), 0
                        states = st[:, bass.ds(i * unroll, unroll + 1)]
                        for k in range(unroll):
                            step(states[:, k], states[:, k + 1])
                    count[0], count[1] = start + 3 * (CHUNK - 1), 0
                    if c < CHUNKS - 1:
                        dve.wait_ge(scan_step, count[0] + 1)
                        dve.tensor_copy(carry, st[:, CHUNK - 1]).then_inc(carried, 1)
                for c in range(4):
                    dve.wait_ge(y_high, c + 1)
                    dve.tensor_tensor(ys[:, 4 * c:4 * c + 4, 1, :], u[:, 4 * c:4 * c + 4],
                                      ys[:, 4 * c:4 * c + 4, 0, :].bitcast(F32), ALU.subtract).then_inc(y_split, 1)

            def forget_gate():
                dve.wait_ge(gate_logits, 1)
                chain.step(dve.tensor_reduce(c16[:, 0], acc[0:HEADS, 0, 0].rearrange("p (h t) -> p t h", h=2),
                                             AX_X, ALU.add))
                chain.wait()
                dve.tensor_tensor(c16[:, 1], c16[:, 0], rstd[0:HEADS], ALU.mult).then_inc(gate_taken, 1)
                dve.wait_ge(gate_taken, 1)
                chain.step(dve.tensor_scalar(c16[:, 0], c16[:, 1], bf_sb[:], None, ALU.add))
                chain.wait()
                dve.scalar_tensor_tensor(c16[:, 3], c16[:, 0], -1.0, c16[:, 0], ALU.mult, ALU.max).then_inc(abs_ready, 1)
                dve.wait_ge(soft_done, 1)
                dve.tensor_scalar(c16[:, 4], c16[:, 2], 1.0, None, ALU.add).then_inc(abs_ready, 1)
                dve.wait_ge(abs_ready, 2)
                chain.step(dve.tensor_scalar(c16[:, 1], c16[:, 4], -1.0, 2.0 ** -24, ALU.add, ALU.max))
                chain.wait()
                dve.wait_ge(soft_done, 2)
                chain.step(dve.reciprocal(c16[:, 4], c16[:, 1]))
                chain.wait()
                chain.step(dve.tensor_tensor(c16[:, 1], c16[:, 2], c16[:, 4], ALU.mult))
                chain.wait()
                chain.step(dve.tensor_tensor(c16[:, 2], c16[:, 1], c16[:, 3], ALU.mult))
                chain.wait()
                chain.step(dve.tensor_scalar(c16[:, 3], c16[:, 0], 0.0, None, ALU.min))
                chain.wait()
                chain.step(dve.tensor_tensor(c16[:, 4], c16[:, 3], c16[:, 2], ALU.subtract))
                chain.step(dve.memset(c16[:, 0], 0.0))
                chain.wait()
                chain.step(dve.tensor_scalar(c16[:, 2], c16[:, 0], 1.0, None, ALU.add))
                chain.wait()
                chain.step(dve.tensor_tensor_scan(c16[:, 1], c16[:, 2], c16[:, 4], 0.0, ALU.mult, ALU.add))
                chain.wait()
                dve.tensor_scalar(c16[:, 0], c16[:, 1], -1.0, None, ALU.mult).then_inc(c_ready, 1)

            def attention():
                dve.wait_ge(cq_taken, 1)
                dve.wait_ge(masks_ready, 1)

                def front(h, b):
                    dve.wait_ge(scores_done, h + 1)
                    if not isinstance(h, int) or h >= 2:
                        dve.wait_ge(probs_turned, h - 1)
                    for qb, cols in ((0, slice(0, P)), (1, slice(P, 3 * P))):
                        chain.step(dve.scalar_tensor_tensor(
                            pr[:, b, cols], acc[:, b, 0, cols], cq[:, qb, bass.ds(h, 1)], mask[:, cols],
                            ALU.add, ALU.add))
                    chain.wait()
                    for qb, cols in ((0, slice(0, P)), (1, slice(P, 3 * P))):
                        ins = dve.tensor_reduce(negmax[:, b, qb:qb + 1], pr[:, b, cols], AX_X, ALU.max, negate=True)
                    ins.then_inc(max_done, 1)

                def back(h, b):
                    dve.wait_ge(exp_done, h + 1)
                    chain.step(dve.reciprocal(row_inv[:, b], row_sum[:, b]))
                    chain.wait()
                    for qb, cols in ((0, slice(0, P)), (1, slice(P, 3 * P))):
                        ins = dve.tensor_scalar(pr[:, b, cols], pr[:, b, cols], row_inv[:, b, qb:qb + 1], None,
                                                ALU.mult)
                    ins.then_inc(probs_ready, 1)

                def last(h, b):
                    dve.wait_ge(o_high, h + 1)
                    head = bass.ds(h, 1)
                    dve.tensor_tensor(os_[:, head, 1, :].rearrange("p o t -> p (o t)"), acc[:, b, 3, 0:SEQ],
                                      os_[:, head, 0, :].rearrange("p o t -> p (o t)").bitcast(F32), ALU.subtract
                                      ).then_inc(o_split, 1)

                front(0, 0)
                front(1, 1)
                back(0, 0)
                with dve.Fori(0, HEADS // 2 - 1) as i:
                    chain.enter(i, 6)
                    for b in range(2):
                        back(i * 2 + (b + 1), 1 - b)
                        front(i * 2 + (b + 2), b)
                        last(i * 2 + b, b)
                chain.leave(HEADS // 2 - 1, 6)
                back(HEADS - 1, 1)
                last(HEADS - 2, 0)
                last(HEADS - 1, 1)

            dve.wait_ge(gains_loaded, 16)

            def bring(c):
                dve.wait_ge(x_loaded[c], 16)
                if c:
                    dve.wait_ge(x_split, c)
                gain(None, 4 * c, 4, GAIN_A).then_inc(gained, 1)
                fin_low(c, 4 * c, 4)

            bring(0)

            def bring_in(slot):
                if slot < 2:
                    bring(2 + slot)

            def discretise(s, slot):
                if (s, slot) == (1, 2):
                    dve.wait_ge(disc_ready, 1)
                    chain.step(dve.tensor_copy(scr_i[:], scr[:, 13]))
                    chain.step(dve.reciprocal(scr[:, 21], scr[:, 20]))
                    chain.wait()
                    dve.tensor_tensor(scr[:, 15], scr[:, 14], scr_i[:].bitcast(F32), ALU.mult
                                      ).then_inc(coef_ready, 1)

            prev = phase(WIN, bring_in)

            for slot in range(3):
                prev(slot)
            s5()
            prev = phase(GLU, lambda slot: None)
            prev = phase(UP0, prev)
            prev = phase(DOWN0, prev)
            prev = phase(KEY, prev)

            def after_key(slot, prev=prev):
                prev(slot)

                def part(c):
                    if c:
                        dve.wait_ge(xq_split, c)
                    else:
                        dve.wait_ge(x_split, DOWN0.fin0 + DOWN0.strips)
                    gain(None, 4 * c, 4, GAIN_B).then_inc(xq_gained, 1)
                    dve.wait_ge(xq_high, c + 1)
                    dve.tensor_tensor(xq[:, 4 * c:4 * c + 4, 1, :], xg[:],
                                      xq[:, 4 * c:4 * c + 4, 0, :].bitcast(F32), ALU.subtract).then_inc(xq_split, 1)

                part(slot)
                if slot == 2:
                    part(3)

            prev = phase(VAL, after_key)

            def after_value(slot, prev=prev):
                prev(slot)
                if slot == 0:
                    forget_gate()

            prev = phase(QRY, after_value)

            def after_query(slot, prev=prev):
                prev(slot)
                if slot == 0:
                    attention()

            prev = phase(WO, after_query)
            prev = phase(UP1, prev)
            prev = phase(DOWN1, prev)
            prev(0)
            rms_inverse(5)
            dve.wait_ge(x_updated, DOWN1.fin0 + DOWN1.strips)
            for c in range(4):
                for j in range(4):
                    kt = 4 * c + j
                    ins = dve.scalar_tensor_tensor(x[:, kt], x[:, kt], g_sb[:, GAIN_FINAL, kt:kt + 1], rstd[:],
                                                   ALU.mult, ALU.mult)
                ins.then_inc(out_ready, 1)

        @block.gpsimd
        def _(pool):
            chain = Chain(pool, pool_chain)

            def do(ins):
                chain.step(ins)
                chain.wait()

            def tt(o, a, b, alu):
                do(pool.tensor_tensor(o, a, b, alu))

            def ts(o, a, s1, op0, s2=None, op1=None):
                do(pool.tensor_scalar(o, a, s1, s2, op0, op1) if op1 else pool.tensor_scalar(o, a, s1, None, op0))

            chain.step(pool.memset(ident[:], 0.0))
            chain.step(pool.memset(eps[:], NORM_EPS))
            chain.wait()
            pool.memset(ones[:], 1.0).then_inc(consts_done, 1)
            pool.affine_select(out=ident[:], in_=ident[:], compare_op=ALU.not_equal, fill=1.0, base=0,
                               pattern=[[-1, P]], channel_multiplier=1).then_inc(consts_done, 1)

            def add_squares(tile, nt):
                for j in range(0, nt, 2):
                    tiles = x[:, bass.ds(tile + j, 2)]
                    tt(square[:], tiles, tiles, ALU.mult)
                    tt(square_sum[:], square_sum[:], square[:, 0], ALU.add)
                    if j == nt - 2:
                        chain.wait()
                        pool.tensor_tensor(square_sum[:], square_sum[:], square[:, 1], ALU.add
                                           ).then_inc(squares_summed, 1)
                    else:
                        tt(square_sum[:], square_sum[:], square[:, 1], ALU.add)

            do(pool.memset(bb[:], 0.0))

            LR, LI, LS = (scr[:, k] for k in range(3))
            T = [scr[:, k] for k in range(30)]
            pool.wait_ge(rates_loaded, 16 * 4)
            MAGIC = 1.5 * 2.0 ** 23
            LN2_HI, LN2_LO = 0.693359375, -2.12194440e-4
            PI = 3.141592653589793
            TAU_1, TAU_2 = 6.28125, 0.0019350051879882812
            TAU_3 = 2 * PI - TAU_1 - TAU_2

            def exp_poly(o, r, tmp):
                coef = [1 / 5040, 1 / 720, 1 / 120, 1 / 24, 1 / 6, 0.5, 1.0, 1.0]
                ts(o, r, coef[0], ALU.mult, coef[1], ALU.add)
                for a in coef[2:]:
                    tt(tmp, o, r, ALU.mult)
                    ts(o, tmp, a, ALU.add)

            def exp_reduce(o_r, o_k, z, tmp):
                ts(tmp, z, -87.0, ALU.max, 88.0, ALU.min)
                ts(o_k, tmp, 1 / 0.6931471805599453, ALU.mult, MAGIC, ALU.add)
                ts(o_k, o_k, -MAGIC, ALU.add)
                ts(o_r, o_k, -LN2_HI, ALU.mult)
                tt(o_r, o_r, tmp, ALU.add)
                ts(tmp, o_k, -LN2_LO, ALU.mult)
                tt(o_r, o_r, tmp, ALU.add)

            exp_reduce(T[3], T[4], LS, T[5])
            exp_poly(T[6], T[3], T[5])
            ts(T[13], T[4], 127.0, ALU.add, 8388608.0, ALU.mult)
            do(pool.tensor_copy(scr_i[:], T[13]))
            tt(T[11], T[6], scr_i[:].bitcast(F32), ALU.mult)
            tt(T[12], LI, T[11], ALU.mult)
            ts(T[3], T[12], 1 / (2 * PI), ALU.mult, MAGIC, ALU.add)
            ts(T[3], T[3], -MAGIC, ALU.add)
            for tau in (TAU_1, TAU_2, TAU_3):
                ts(T[4], T[3], -tau, ALU.mult)
                tt(T[12], T[12], T[4], ALU.add)
            ts(T[7], T[12], 3.1415925, ALU.min, -3.1415925, ALU.max)
            ts(T[3], T[12], PI / 2, ALU.is_gt)
            ts(T[3], T[3], -2 * PI, ALU.mult, PI / 2, ALU.add)
            tt(T[4], T[12], T[3], ALU.add)
            chain.wait()
            pool.tensor_scalar(T[9], T[4], 3.1415925, -3.1415925, ALU.min, ALU.max).then_inc(angle_ready, 1)
            rows = squares_in[:, 0:4]
            for c in range(1, 4):
                pool.wait_ge(squared, c + 1)
                tt(rows, rows, squares_in[:, 4 * c:4 * c + 4], ALU.add)
            tt(rows[:, 0:2], rows[:, 0:2], rows[:, 2:4], ALU.add)
            pool.tensor_tensor(square_sum[:], rows[:, 0], rows[:, 1], ALU.add).then_inc(squares_summed, 4)
            pool.wait_ge(squares_summed, 4)
            pool.memset(c_pad[:], 0.0).then_inc(c_cleared, 1)
            tt(T[16], LR, T[11], ALU.mult)
            exp_reduce(T[3], T[4], T[16], T[5])
            exp_poly(T[14], T[3], T[5])
            ts(T[13], T[4], 127.0, ALU.add, 8388608.0, ALU.mult)
            tt(T[17], LR, LR, ALU.mult)
            tt(T[18], LI, LI, ALU.mult)
            chain.wait()
            pool.tensor_tensor(T[20], T[17], T[18], ALU.add).then_inc(disc_ready, 1)
            pool.wait_ge(coef_ready, 1)
            pool.wait_ge(trig_done, 1)
            pool.wait_ge(x_split, 4)
            LAM_RE, LAM_IM, LAM_NEG = (xg[:, 3, k * PAIRS:(k + 1) * PAIRS] for k in range(3))
            tt(LAM_RE, T[15], T[10], ALU.mult)
            tt(LAM_IM, T[15], T[8], ALU.mult)
            ts(LAM_NEG, LAM_IM, -1.0, ALU.mult)
            tt(T[22], LAM_RE, LAM_RE, ALU.mult)
            tt(T[23], LAM_IM, LAM_IM, ALU.mult)
            tt(a4[:, 0, 0], T[22], T[23], ALU.subtract)
            chain.step(pool.tensor_copy(a4[:, 1, 1], a4[:, 0, 0]))
            tt(T[24], LAM_RE, LAM_IM, ALU.mult)
            ts(a4[:, 0, 1], T[24], -2.0, ALU.mult)
            pool.tensor_scalar(a4[:, 1, 0], T[24], 2.0, None, ALU.mult).then_inc(disc_taken, 1)
            ts(T[3], LAM_RE, -1.0, ALU.add)
            for o, a, b, alu in ((28, T[3], LAM_IM, ALU.add), (29, LAM_IM, T[3], ALU.subtract)):
                tt(T[25], a, LR, ALU.mult)
                tt(T[26], b, LI, ALU.mult)
                tt(T[27], T[25], T[26], alu)
                tt(T[o], T[27], T[21], ALU.mult)
            for o, a, b, alu in ((6, LAM_RE, LAM_IM, ALU.subtract), (7, LAM_IM, LAM_RE, ALU.add)):
                tt(T[25], T[28], a, ALU.mult)
                tt(T[26], T[29], b, ALU.mult)
                tt(T[o], T[25], T[26], alu)

            def wide(ap):
                return ap.unsqueeze(2).to_broadcast([P, PAIRS, GROUP])

            def own_groups(g2):
                return slice(64 * g2, 64 * g2 + 64)

            pool.wait_ge(params_loaded, 16 * 6)
            for power, re, im in ((1, T[28], T[29]), (0, T[6], T[7])):
                for ri, b0, b1, alu in ((0, 0, 1, ALU.subtract), (1, 1, 0, ALU.add)):
                    tt(prod[:, 0], b_nat[:, b0], wide(re), ALU.mult)
                    tt(prod[:, 1], b_nat[:, b1], wide(im), ALU.mult)
                    for g2 in range(2):
                        half = own_groups(g2)
                        dst = bb[half, :, :, ri, :, power, g2 * GROUP:(g2 + 1) * GROUP]
                        do(pool.tensor_tensor(dst.rearrange("p m e b c -> p (m e) b c"),
                                              prod[half, 0].rearrange("p (n b) c -> p n b c", b=2),
                                              prod[half, 1].rearrange("p (n b) c -> p n b c", b=2), alu))

            pool.wait_ge(c_cleared, 1)
            pool.memset(kd[:], 0.0).then_inc(b_bar_ready, 1)
            pool.wait_ge(w_split, HALVES * (RING + WIN.strips * WIN.kc))
            pool.wait_ge(weights_used, HALVES * (RING + WIN.strips * WIN.kc))
            pool.wait_ge(scaled, WIN.strips)
            do(pool.memset(cb[:, 1], 0.0))
            part = PAIRS // 4
            for ri, by_re, by_im in ((0, LAM_RE, LAM_IM), (1, LAM_NEG, LAM_RE)):
                for q0 in range(0, PAIRS, part):
                    qs = slice(q0, q0 + part)
                    prods = [reduced[:, 2 + k].rearrange("p (q c) -> p q c", c=GROUP) for k in range(2)]
                    tt(prods[0], c_nat[:, 0, qs], by_re[:, qs].unsqueeze(2).to_broadcast([P, part, GROUP]), ALU.mult)
                    tt(prods[1], c_nat[:, 1, qs], by_im[:, qs].unsqueeze(2).to_broadcast([P, part, GROUP]), ALU.mult)
                    for g2 in range(2):
                        half = own_groups(g2)
                        do(pool.tensor_tensor(cb[half, 1, ri, qs, g2, :], prods[0][half], prods[1][half],
                                              ALU.subtract))
            pool.tensor_tensor(dg[:], ident[:].unsqueeze(1).to_broadcast([P, KT, P]),
                               d_sb[:].unsqueeze(2).to_broadcast([P, KT, P]), ALU.mult).then_inc(s5_mats_ready, 1)
            pool.wait_ge(s5_filled, 5 + 4 * CHUNKS + 2 * CHUNKS)
            do(pool.memset(gate[:, :, 0:2], 0.0))

            def clear_squares(n):
                pool.wait_ge(norm_summed, n)
                do(pool.memset(square_sum[:], 0.0))

            def squares(ph, nt, per):
                def body(s, par):
                    pool.wait_ge(x_updated, ph.fin0 + s + 1)
                    reach(pool, squares_summed, ph.fin0 + s)
                    add_squares(s * nt, nt)

                pairs_of_strips(pool, ph, body, chain, per)

            def up(ph):
                def body(s, par):
                    n = ph.up0 + s
                    if isinstance(s, int) and s == 0:
                        pool.wait_ge(rstd_done, ph.norm)
                    pool.wait_ge(strip_reduced, ph.strip0 + s + 3)
                    reach(pool, hidden_split, n)
                    pool.tensor_tensor(value[:], reduced[:, 2:4], rstd[:].unsqueeze(1).to_broadcast([P, 2, SEQ]),
                                       ALU.mult).then_inc(value_scaled, 1)
                    pool.wait_ge(value_scaled, n + 1)
                    pool.wait_ge(gelu_done, n + 1)
                    pool.tensor_tensor(value[:], value[:], conv_acc[:], ALU.mult).then_inc(hidden_ready, 1)
                    pool.wait_ge(hidden_high, n + 1)
                    tiles = bass.ds(s * 2, 2)
                    pool.tensor_tensor(hs[:, tiles, 1, :], value[:], hs[:, tiles, 0, :].bitcast(F32), ALU.subtract
                                       ).then_inc(hidden_split, 1)

                pairs_of_strips(pool, ph, body)

            clear_squares(1)
            squares(GLU, 2, 2 * 2)
            up(UP0)
            clear_squares(2)
            squares(DOWN0, 4, 2 * 5)
            pool.wait_ge(scaled, KEY.scale0 + 1)
            do(pool.memset(mask[:], 0.0))
            for cols, base in ((slice(0, P), 0), (slice(P, 3 * P), P)):
                do(pool.affine_select(out=mask[:, cols], in_=mask[:, cols], compare_op=ALU.is_ge, fill=MASKED,
                                      base=base, pattern=[[-1, cols.stop - cols.start]], channel_multiplier=1))
            do(pool.memset(e16[:], 0.0))
            pool.affine_select(out=e16[:], in_=e16[:], compare_op=ALU.not_equal, fill=1.0, base=0,
                               pattern=[[-1, HEADS]], channel_multiplier=1).then_inc(masks_ready, 1)

            pool.wait_ge(masks_ready, 1)
            pool.wait_ge(c_ready, 1)
            pool.wait_ge(scaled, QRY.scale0 + QRY.strips)

            def stage(h, b):
                if not isinstance(h, int) or h >= 2:
                    pool.wait_ge(v_turned, h - 1)
                head = bass.ds(h, 1)
                chain.step(pool.tensor_copy(q_st[:, b], qT[:, head].rearrange("p o t -> p (o t)")))
                chain.step(pool.tensor_copy(v_st[:, b], vT[:, head].rearrange("p o t -> p (o t)")))
                pool.tensor_tensor(ck_st[:, b], c16[:, 0], e16[:, head].to_broadcast([HEADS, SEQ]), ALU.mult
                                   ).then_inc(head_staged, 1)

            stage(0, 0)
            stage(1, 1)
            with pool.Fori(0, HEADS // 2 - 1) as i:
                chain.enter(i, 4)
                stage(i * 2 + 2, 0)
                stage(i * 2 + 3, 1)
            chain.leave(HEADS // 2 - 1, 4)
            pool.wait_ge(scores_done, HEADS)
            pool.wait_ge(o_split, HEADS + 2)
            do(pool.memset(gate[:, :, 0:2], 0.0))
            clear_squares(3)
            squares(WO, 4, 2 * 5)
            up(UP1)
            clear_squares(4)
            squares(DOWN1, 4, 2 * 5)


def kernel(**inputs):
    import numpy as np
    import concourse.bacc as bacc
    from concourse.bass_utils import run_bass_kernel_spmd as run

    a = {k: np.asarray(v) for k, v in inputs.items()}

    def plain(w):
        k, n = w.shape
        return np.ascontiguousarray(w.reshape(k // 512, 4, P, n // 512, 512).transpose(3, 0, 2, 1, 4)
                                    ).reshape(-1, P, 2048)

    def paired(w):
        k, n = w.shape
        return np.ascontiguousarray(w.reshape(k // 512, 4, P, 2, n // 512, 256).transpose(4, 0, 2, 1, 3, 5)
                                    ).reshape(-1, P, 2048)

    def columns(v):
        return v.reshape(-1, P).T

    w_up = a["ffn_w_up"]
    arrays = {
        "xT": a["x"][0].T.reshape(KT, P, SEQ).transpose(1, 0, 2),
        "gains": np.stack([columns(v) for v in (a["a_norm"][0], a["ffn_norm"][0], a["kv_norm"], a["b_norm"][0],
                                                a["ffn_norm"][1], a["final_norm"])], axis=1),
        "w_in": plain(a["a_w_in"][0]),
        "w_glu": paired(a["a_w_glu"][0]),
        "w_k": plain(a["w_k"]),
        "w_v": plain(a["w_v"]),
        "w_f": a["w_f"].reshape(KT, P, HEADS).transpose(1, 0, 2),
        "b_f": a["b_f"].reshape(HEADS, 1),
        "w_q": plain(a["b_w_q"][0]),
        "w_o": plain(a["b_w_o"][0]),
        "w_up": np.concatenate([paired(w) for w in w_up]),
        "w_down": np.concatenate([plain(w) for w in a["ffn_w_down"]]),
        "conv": np.stack([np.stack([columns(v) for v in (*a["ffn_conv_w"][l], a["ffn_conv_b"][l])], axis=1)
                          for l in range(2)], axis=1),
        "skip_d": columns(a["a_d"][0].reshape(-1)),
        "lam": np.stack([columns(a["a_lambda_re"][0].reshape(-1)), columns(a["a_lambda_im"][0].reshape(-1))], axis=1),
        "log_step": a["a_log_step"][0].reshape(PAIRS, 2).T,
        "b_in": np.stack([a[n][0].reshape(PAIRS, P, GROUP).transpose(1, 0, 2) for n in ("a_b_re", "a_b_im")], axis=1),
        "c_out": np.stack([a[n][0].reshape(PAIRS, 2, GROUP, STATE).transpose(1, 3, 0, 2).reshape(P, PAIRS, GROUP)
                           for n in ("a_c_re", "a_c_im")], axis=1),
    }
    arrays = {k: np.ascontiguousarray(v) for k, v in arrays.items()}
    nc = bacc.Bacc("TRN2", target_bir_lowering=False, num_devices=1)
    args = [nc.dram_tensor(n, v.shape, F32, kind="ExternalInput").ap() for n, v in arrays.items()]
    names = list(arrays)
    by = dict(zip(names, args))
    o = nc.dram_tensor("out", (P, KT, SEQ), F32, kind="ExternalOutput").ap()
    trunk(nc, **by, out=o)
    r = run(nc, [arrays], core_ids=[0])
    got = r.results[0]["out"]
    return np.ascontiguousarray(got.transpose(1, 0, 2).reshape(D_MODEL, SEQ).T)[None]
```
